# Optimizing a Trainium2 kernel written in Bass

```python
import jax, jax.numpy as jnp
from jax import lax
import numpy as np

D_MODEL = 1024
BATCH = 1
SEQ = 256
DEPTH = 2

RET_HEADS = 4
RET_DK = 128
RET_DV = 128
RET_CHUNK = 128
ROPE_BASE = 10000.0
RET_QK_W = RET_HEADS * RET_DK
RET_V_W = RET_HEADS * RET_DV
POOL_WINDOWS = (2, 4, 8, 16)
POOL_GROUPS = 4
POOL_GROUP_DIM = 128
POOL_W = POOL_GROUPS * POOL_GROUP_DIM
SSM_HEADS = 16
SSM_HEAD_DIM = 64
SSM_INNER = SSM_HEADS * SSM_HEAD_DIM
SSM_GROUPS = 2
SSM_STATE = 128
SSM_CONV = 4
SSM_CHUNK = 128
SSM_XBC = SSM_INNER + 2 * SSM_GROUPS * SSM_STATE
FOX_HEADS = 4
FOX_HEAD_DIM = 128
FOX_BLOCK = 128
FOX_W = FOX_HEADS * FOX_HEAD_DIM
N_BRANCH = 4
D_FF = 2816
N_SUBLAYERS = 3
RMS_EPS = 1e-6
GN_EPS = 1e-5
IN_SIZES = (RET_QK_W, RET_QK_W, RET_V_W, RET_V_W, POOL_W, SSM_INNER, SSM_XBC, SSM_HEADS, FOX_W, FOX_W, FOX_W, FOX_HEADS, N_BRANCH * D_MODEL)
IN_WIDTH = 2 * RET_QK_W + 2 * RET_V_W + POOL_W + SSM_INNER + SSM_XBC + SSM_HEADS + 3 * FOX_W + FOX_HEADS + N_BRANCH * D_MODEL

kernel_name = "hybrid_gated_ret_pool_ssd_fox_macaron"

F32 = jnp.float32

def rms_norm(x, gain):
    x32 = x.astype(F32)
    y = x32 * lax.rsqrt(jnp.mean(x32 * x32, axis=-1, keepdims=True) + RMS_EPS)
    return (y * gain.astype(F32)).astype(x.dtype)

def modulate(h, shift, scale):
    return h * (1 + scale[:, None, :]) + shift[:, None, :]

def swiglu_ffn(h, w_in, w_out):
    g, u = jnp.split(h @ w_in, 2, axis=-1)
    return (jax.nn.silu(g) * u) @ w_out

def rotary(x, pos):
    half = x.shape[-1] // 2
    inv = ROPE_BASE ** (-jnp.arange(half, dtype=F32) / half)
    ang = pos.astype(F32)[:, None] * inv[None, :]
    cos = jnp.cos(ang)[None, :, None, :]
    sin = jnp.sin(ang)[None, :, None, :]
    x1 = x[..., :half].astype(F32)
    x2 = x[..., half:].astype(F32)
    return jnp.concatenate([x1 * cos - x2 * sin, x1 * sin + x2 * cos], axis=-1)

def head_group_norm(o):
    mu = jnp.mean(o, axis=-1, keepdims=True)
    var = jnp.mean(jnp.square(o - mu), axis=-1, keepdims=True)
    return (o - mu) * lax.rsqrt(var + GN_EPS)

def retention_chunkwise(q, k, v):
    bsz, seq, nh, dk = q.shape
    dv = v.shape[-1]
    cl = RET_CHUNK
    n = seq // cl
    log_gamma = jnp.log1p(-jnp.exp2(-5.0 - jnp.arange(nh, dtype=F32)))
    idx = jnp.arange(cl, dtype=F32)
    rel = idx[:, None] - idx[None, :]
    intra_decay = jnp.where(rel >= 0, jnp.exp(log_gamma[:, None, None] * jnp.maximum(rel, 0.0)), 0.0)
    q_decay = jnp.exp(log_gamma[:, None] * (idx + 1.0))
    k_decay = jnp.exp(log_gamma[:, None] * (cl - 1.0 - idx))
    chunk_decay = jnp.exp(log_gamma * cl)

    def to_chunks(t):
        return t.reshape(bsz, n, cl, nh, t.shape[-1]).transpose(1, 0, 3, 2, 4)

    def step(state, inp):
        qc, kc, vc = inp
        scores = jnp.einsum('bhid,bhjd->bhij', qc, kc) * intra_decay
        o = jnp.einsum('bhij,bhje->bhie', scores, vc) + jnp.einsum('bhid,bhde->bhie', qc, state) * q_decay[:, :, None]
        state = chunk_decay[:, None, None] * state + jnp.einsum('bhjd,bhje->bhde', kc * k_decay[:, :, None], vc)
        return state, o

    s0 = jnp.zeros((bsz, nh, dk, dv), F32)
    _, o = lax.scan(step, s0, (to_chunks(q), to_chunks(k), to_chunks(v)))
    return o.transpose(1, 0, 3, 2, 4).reshape(bsz, seq, nh, dv)

def pool_mixer(u, w_pool, pool_scale):
    bsz, seq, _ = u.shape
    u32 = u.reshape(bsz, seq, POOL_GROUPS, POOL_GROUP_DIM).astype(F32)
    cs = jnp.pad(jnp.cumsum(u32, axis=1), ((0, 0), (1, 0), (0, 0), (0, 0)))
    t = jnp.arange(seq)
    win = jnp.array(POOL_WINDOWS, dtype=jnp.int32)
    lo = jnp.maximum(t[:, None] + 1 - win[None, :], 0)
    g_idx = jnp.arange(POOL_GROUPS)[None, :]
    lo_sum = cs[:, lo, g_idx]
    count = (t[:, None] + 1 - lo).astype(F32)
    pooled = (cs[:, 1:] - lo_sum) / count[None, :, :, None] - u32
    mixed = jnp.einsum('blgc,gcd->blgd', pooled.astype(u.dtype), w_pool)
    return mixed.reshape(bsz, seq, POOL_W) * pool_scale

def causal_depthwise_conv(u, w, b):
    out = lax.conv_general_dilated(u, w[:, None, :].astype(u.dtype), window_strides=(1,), padding=[(SSM_CONV - 1, 0)], dimension_numbers=('NWC', 'WIO', 'NWC'), feature_group_count=u.shape[-1])
    return out + b

def ssd_scan(x, dt, a, bm, cm):
    bsz, seq, nh, hp = x.shape
    ng = bm.shape[2]
    hg = nh // ng
    cl = SSM_CHUNK
    n = seq // cl
    da = dt * a
    xdt = x * dt[..., None]
    causal = jnp.tril(jnp.ones((cl, cl), dtype=bool))

    def chunks(t):
        return t.reshape((bsz, n, cl) + t.shape[2:]).swapaxes(0, 1)

    def step(state, inp):
        xc, dac, bc, cc = inp
        acum = jnp.cumsum(dac, axis=1)
        seg = acum[:, :, None, :] - acum[:, None, :, :]
        lmat = jnp.exp(jnp.where(causal[None, :, :, None], seg, -jnp.inf)).reshape(bsz, cl, cl, ng, hg)
        cb = jnp.einsum('bign,bjgn->bijg', cc, bc)
        xg = xc.reshape(bsz, cl, ng, hg, hp)
        y = jnp.einsum('bijgh,bjghp->bighp', lmat * cb[..., None], xg)
        acum_g = acum.reshape(bsz, cl, ng, hg)
        y = y + jnp.einsum('bign,bghpn->bighp', cc, state) * jnp.exp(acum_g)[..., None]
        decay_end = jnp.exp(acum_g[:, -1:] - acum_g)
        state = jnp.exp(acum_g[:, -1])[..., None, None] * state + jnp.einsum('bjgn,bjgh,bjghp->bghpn', bc, decay_end, xg)
        return state, y.reshape(bsz, cl, nh, hp)

    s0 = jnp.zeros((bsz, ng, hg, hp, bm.shape[-1]), F32)
    _, y = lax.scan(step, s0, (chunks(xdt), chunks(da), chunks(bm), chunks(cm)))
    return y.swapaxes(0, 1).reshape(bsz, seq, nh, hp)

def ssd_mixer(z, xbc, dt_raw, conv_w, conv_b, dt_bias, a_log, d_skip, norm_w):
    bsz, seq, _ = z.shape
    xbc = jax.nn.silu(causal_depthwise_conv(xbc, conv_w, conv_b))
    xs, bm, cm = jnp.split(xbc, [SSM_INNER, SSM_INNER + SSM_GROUPS * SSM_STATE], axis=-1)
    xs = xs.reshape(bsz, seq, SSM_HEADS, SSM_HEAD_DIM).astype(F32)
    bm = bm.reshape(bsz, seq, SSM_GROUPS, SSM_STATE).astype(F32)
    cm = cm.reshape(bsz, seq, SSM_GROUPS, SSM_STATE).astype(F32)
    dt = jax.nn.softplus(dt_raw.astype(F32) + dt_bias.astype(F32))
    a = -jnp.exp(a_log.astype(F32))
    y = ssd_scan(xs, dt, a, bm, cm) + d_skip.astype(F32)[:, None] * xs
    y = y.reshape(bsz, seq, SSM_INNER).astype(z.dtype)
    return rms_norm(y * jax.nn.silu(z), norm_w)

def forgetting_attention(q, k, v, log_f):
    bsz, seq, nh, hd = q.shape
    nb = seq // FOX_BLOCK
    cum = jnp.cumsum(log_f, axis=1).transpose(0, 2, 1)
    qh = (q.astype(F32) * (hd ** -0.5)).transpose(0, 2, 1, 3)
    kh = k.astype(F32).transpose(0, 2, 1, 3)
    vh = v.astype(F32).transpose(0, 2, 1, 3)
    qb = qh.reshape(bsz, nh, nb, FOX_BLOCK, hd).transpose(2, 0, 1, 3, 4)
    cb = cum.reshape(bsz, nh, nb, FOX_BLOCK).transpose(2, 0, 1, 3)
    kpos = jnp.arange(seq)

    def block(inp):
        qi, ci, i = inp
        s = jnp.einsum('bhqd,bhkd->bhqk', qi, kh) + ci[..., None] - cum[:, :, None, :]
        qpos = i * FOX_BLOCK + jnp.arange(FOX_BLOCK)
        s = jnp.where(kpos[None, :] <= qpos[:, None], s, -jnp.inf)
        p = jax.nn.softmax(s, axis=-1)
        return jnp.einsum('bhqk,bhkd->bhqd', p, vh)

    o = lax.map(block, (qb, cb, jnp.arange(nb)))
    return o.transpose(1, 0, 3, 2, 4).reshape(bsz, seq, nh * hd).astype(q.dtype)

def hybrid_mixer(h, w_in, b_forget, pool_w, pool_scale, conv_w, conv_b, dt_bias, a_log, d_skip, ssm_norm, w_ret_out, w_pool_out, w_ssm_out, w_fox_out, w_out):
    bsz, seq, _ = h.shape
    proj = h @ w_in
    points = [int(p) for p in np.cumsum(IN_SIZES)[:-1]]
    rq, rk, rv, rg, pu, sz, sxbc, sdt, fq, fk, fv, ff, gl = jnp.split(proj, points, axis=-1)
    pos = jnp.arange(seq)
    rq = rotary(rq.reshape(bsz, seq, RET_HEADS, RET_DK), pos)
    rk = rotary(rk.reshape(bsz, seq, RET_HEADS, RET_DK), pos) * (RET_DK ** -0.5)
    ret = retention_chunkwise(rq, rk, rv.reshape(bsz, seq, RET_HEADS, RET_DV).astype(F32))
    y_a = jax.nn.silu(rg) * head_group_norm(ret).reshape(bsz, seq, RET_V_W).astype(h.dtype)
    y_b = pool_mixer(pu, pool_w, pool_scale)
    y_c = ssd_mixer(sz, sxbc, sdt, conv_w, conv_b, dt_bias, a_log, d_skip, ssm_norm)
    log_f = jax.nn.log_sigmoid(ff.astype(F32) + b_forget.astype(F32))
    y_d = forgetting_attention(fq.reshape(bsz, seq, FOX_HEADS, FOX_HEAD_DIM), fk.reshape(bsz, seq, FOX_HEADS, FOX_HEAD_DIM), fv.reshape(bsz, seq, FOX_HEADS, FOX_HEAD_DIM), log_f)
    gates = jax.nn.sigmoid(gl.reshape(bsz, seq, N_BRANCH, D_MODEL))
    merged = (gates[:, :, 0] * (y_a @ w_ret_out) + gates[:, :, 1] * (y_b @ w_pool_out)
              + gates[:, :, 2] * (y_c @ w_ssm_out) + gates[:, :, 3] * (y_d @ w_fox_out))
    return merged @ w_out

def setup_inputs(seed: int = 0) -> dict:
    key = jax.random.key(seed)
    ks = jax.random.split(key, 24)
    nrm = jax.random.normal
    L, D = DEPTH, D_MODEL
    dt0 = jnp.exp(jax.random.uniform(ks[15], (L, SSM_HEADS), minval=np.log(1e-3), maxval=np.log(1e-1)))
    return {
        "x": nrm(ks[0], (BATCH, SEQ, D), F32),
        "c": nrm(ks[1], (BATCH, D), F32),
        "w_ada": nrm(ks[2], (L, D, 3 * N_SUBLAYERS * D), F32) * D ** -0.5,
        "b_ada": nrm(ks[3], (L, 3 * N_SUBLAYERS * D), F32) * 0.01,
        "norm_pre": 1.0 + 0.05 * nrm(ks[4], (L, N_SUBLAYERS, D), F32),
        "norm_post": 1.0 + 0.05 * nrm(ks[5], (L, N_SUBLAYERS, D), F32),
        "w_ffn_in": nrm(ks[6], (L, 2, D, 2 * D_FF), F32) * D ** -0.5,
        "w_ffn_out": nrm(ks[7], (L, 2, D_FF, D), F32) * D_FF ** -0.5,
        "w_in": nrm(ks[8], (L, D, IN_WIDTH), F32) * D ** -0.5,
        "b_forget": 2.0 + 0.5 * nrm(ks[9], (L, FOX_HEADS), F32),
        "pool_w": nrm(ks[10], (L, POOL_GROUPS, POOL_GROUP_DIM, POOL_GROUP_DIM), F32) * POOL_GROUP_DIM ** -0.5,
        "pool_scale": 1.0 + 0.1 * nrm(ks[11], (L, POOL_W), F32),
        "conv_w": nrm(ks[12], (L, SSM_CONV, SSM_XBC), F32) * SSM_CONV ** -0.5,
        "conv_b": nrm(ks[13], (L, SSM_XBC), F32) * 0.01,
        "dt_bias": dt0 + jnp.log(-jnp.expm1(-dt0)),
        "a_log": jnp.log(jax.random.uniform(ks[14], (L, SSM_HEADS), minval=1.0, maxval=16.0)),
        "d_skip": 1.0 + 0.1 * nrm(ks[16], (L, SSM_HEADS), F32),
        "ssm_norm": 1.0 + 0.05 * nrm(ks[17], (L, SSM_INNER), F32),
        "w_ret_out": nrm(ks[18], (L, RET_V_W, D), F32) * RET_V_W ** -0.5,
        "w_pool_out": nrm(ks[19], (L, POOL_W, D), F32) * POOL_W ** -0.5,
        "w_ssm_out": nrm(ks[20], (L, SSM_INNER, D), F32) * SSM_INNER ** -0.5,
        "w_fox_out": nrm(ks[21], (L, FOX_W, D), F32) * FOX_W ** -0.5,
        "w_out": nrm(ks[22], (L, D, D), F32) * D ** -0.5,
    }

def reference(x, c, w_ada, b_ada, norm_pre, norm_post, w_ffn_in, w_ffn_out, w_in, b_forget, pool_w, pool_scale, conv_w, conv_b, dt_bias, a_log, d_skip, ssm_norm, w_ret_out, w_pool_out, w_ssm_out, w_fox_out, w_out):
    for i in range(DEPTH):
        mod = jax.nn.silu(c) @ w_ada[i] + b_ada[i]
        sh1, sc1, g1, sh2, sc2, g2, sh3, sc3, g3 = jnp.split(mod, 3 * N_SUBLAYERS, axis=-1)
        h = modulate(rms_norm(x, norm_pre[i, 0]), sh1, sc1)
        y = swiglu_ffn(h, w_ffn_in[i, 0], w_ffn_out[i, 0])
        x = x + 0.5 * g1[:, None, :] * rms_norm(y, norm_post[i, 0])
        h = modulate(rms_norm(x, norm_pre[i, 1]), sh2, sc2)
        y = hybrid_mixer(h, w_in[i], b_forget[i], pool_w[i], pool_scale[i], conv_w[i], conv_b[i], dt_bias[i], a_log[i], d_skip[i], ssm_norm[i], w_ret_out[i], w_pool_out[i], w_ssm_out[i], w_fox_out[i], w_out[i])
        x = x + g2[:, None, :] * rms_norm(y, norm_post[i, 1])
        h = modulate(rms_norm(x, norm_pre[i, 2]), sh3, sc3)
        y = swiglu_ffn(h, w_ffn_in[i, 1], w_ffn_out[i, 1])
        x = x + 0.5 * g3[:, None, :] * rms_norm(y, norm_post[i, 2])
    return x


_drawn_inputs = setup_inputs


def setup_inputs(seed=0):
    import zlib

    import numpy as np

    out = dict(_drawn_inputs(seed))
    spreads = {}
    factors = {'conv_b': 8.0, 'd_skip': 3.166, 'ssm_norm': 3.044, 'b_ada': 2.692, 'pool_scale': 2.704}
    for name, (base, spread) in spreads.items():
        noise = np.random.default_rng([zlib.crc32(name.encode()), seed]).standard_normal(out[name].shape)
        drawn = base * np.exp(spread * noise) if base else spread * noise
        out[name] = __import__('jax').numpy.asarray(drawn.astype(out[name].dtype))
    for name, factor in factors.items():
        out[name] = (out[name] * factor).astype(out[name].dtype)
    return out
```

```python
from contextlib import ExitStack

import numpy as np

import concourse.bass as bass
from concourse import mybir

F32 = mybir.dt.float32
F32R = mybir.dt.float32r
I32 = mybir.dt.int32
ACT = mybir.ActivationFunctionType
ALU = mybir.AluOpType
AX_X = mybir.AxisListType.X

P = 128
D = 1024
T = 256
TT = T // P
KD = D // P
DEPTH = 2
SUBS = 3
FF = 2816
KF = FF // P
HEADS = 4
SH = 16
SHD = 64
COLS = 256
RMS_EPS = 1e-6
GN_EPS = 1e-5
NEG = -1e30

IN_PAIRS = KF // 2
OUT_SPLIT = (6, 6, 5, 5)
OUT_START = (0, 6, 12, 17)
FFN_UNITS = 2 * IN_PAIRS + 4 * 4
MIX_UNITS = 64
UNITS = 2 * FFN_UNITS + MIX_UNITS
UB_MIX = FFN_UNITS
UB_FFN = (0, FFN_UNITS + MIX_UNITS)
OB_MIX = IN_PAIRS + 2
OB_FFN = (0, OB_MIX + MIX_UNITS // 2)
OUTS = 2 * (IN_PAIRS + 2) + MIX_UNITS // 2
OB_NEXT = (OB_MIX, OB_FFN[1], OUTS)
KEEP = (2, 2, 1, 4)

C_RQ, C_RK, C_RV, C_RG, C_PU, C_SZ, C_XBC, C_DT, C_FQ, C_FK, C_FV, C_FF, C_GL = (
    0, 512, 1024, 1536, 2048, 2560, 3584, 5120, 5136, 5648, 6160, 6672, 6676)

MIX = ([("pu", C_PU + COLS * j, KD, COLS) for j in range(2)]
       + [("dt", C_DT, KD, 16), ("ff", C_FF, KD, 4)]
       + [("xbc", C_XBC + COLS * j, KD, COLS) for j in range(6)]
       + [("fq", C_FQ + COLS * j, KD, COLS) for j in range(2)]
       + [("fk", C_FK + COLS * j, KD, COLS) for j in range(2)]
       + [("fv", C_FV + COLS * j, KD, COLS) for j in range(2)]
       + [("sz", C_SZ + COLS * j, KD, COLS) for j in range(4)])
for _b, _k in ((1, 4), (None, 0), (2, 8), (3, 4), (0, 4)):
    if _b is None:
        MIX += ([("rq", C_RQ + COLS * j, KD, COLS) for j in range(2)]
                + [("rk", C_RK + COLS * j, KD, COLS) for j in range(2)]
                + [("rv", C_RV + COLS * j, KD, COLS) for j in range(2)]
                + [("rg", C_RG + COLS * j, KD, COLS) for j in range(2)])
        continue
    for _p in range(4):
        MIX += [("gate", C_GL + _b * D + _p * COLS, KD, COLS), (("ret", "pool", "ssm", "fox")[_b], _p * COLS, _k, COLS)]
MIX += [("wout", COLS * j, KD, COLS) for j in range(4)]
assert len(MIX) == MIX_UNITS
BRANCHES = ("ret", "pool", "ssm", "fox")
FEATURE_ROWS = ("fv", "rv", "dt", "ff")

K_ID, K_NEGT, K_ZERO, K_NEGF, K_T0, K_T1, K_COS, K_SIN, K_FIX, K_MEAN, K_ONE, K_DEC = (
    0, 128, 256, 384, 512, 640, 768, 1024, 1280, 1344, 1472, 1474)
K_N = K_DEC + HEADS * 384
V_BADA, V_PRE, V_POST, V_SSMN, V_PSC, V_CB, V_CW, V_B20, V_ALOG, V_DSK = (0, 72, 96, 120, 128, 132, 144, 192, 212, 228)
V_N = 236

POOL_SPLITS = range(UB_MIX + 6, UB_MIX + 12)

ADA_STEPS = 16
ADA_COLS = 768
ADA_AT = (10, 11, 13, 15, 28, 30, 32, 34, 36, 37, 39, 41, 42, 43, 45, 46)


def constant_table():
    t = np.zeros((P, K_N), np.float32)
    r = np.arange(P)
    j, i = r[:, None], r[None, :]
    t[:, K_ID:K_ID + P] = np.eye(P)
    t[:, K_NEGT:K_NEGT + P] = np.where(i < j, NEG, 0.0)
    t[:, K_NEGF:K_NEGF + P] = np.where(i > j, NEG, 0.0)
    t[:, K_T0:K_T0 + P] = np.where(j > i, -1.0, 0.0)
    t[:, K_T1:K_T1 + P] = np.where(j <= i, 1.0, 0.0)
    half = P // 2
    inv = 10000.0 ** (-np.arange(half, dtype=np.float64) / half)
    ang = np.arange(T)[None, :] * inv.astype(np.float32).astype(np.float64)[:, None]
    t[:, K_COS:K_COS + T] = np.concatenate([np.cos(ang), np.cos(ang)], 0)
    t[:, K_SIN:K_SIN + T] = np.concatenate([-np.sin(ang), np.sin(ang)], 0)
    for g in range(4):
        w = 2 ** (g + 1)
        t[:, K_FIX + 16 * g:K_FIX + 16 * g + 16] = w / np.minimum(np.arange(16) + 1, w)
    t[:, K_MEAN:K_MEAN + P] = 1.0 / P
    t[:, K_ONE:K_ONE + 2] = 1.0
    for h in range(HEADS):
        gamma = 1.0 - 2.0 ** (-5.0 - h)
        q = np.arange(T)[None, :]
        for off, jj, qq in ((0, j, q), (T, j + P, q[:, P:])):
            rel = (qq - jj).astype(np.float64)
            blk = np.where(rel >= 0, gamma ** np.maximum(rel, 0.0), 0.0) * P ** -0.5
            t[:, K_DEC + 384 * h + off:K_DEC + 384 * h + off + blk.shape[1]] = blk
    return t


class Signal:

    def __init__(self, sem, per_layer, before=0):
        self.sem, self.per_layer, self.before = sem, per_layer, before

    def at(self, layer, n):
        return layer * self.per_layer + (n + self.before)


class Chain:

    def __init__(self, eng, sem, per_layer):
        self.eng, self.sem, self.per_layer, self.base, self.n = eng, sem, per_layer, 0, 0

    def __call__(self, ins):
        self.n += 1
        ins.then_inc(self.sem, 1)
        self.eng.wait_ge(self.sem, self.base + self.n)

    def enter_layers(self, layer):
        self.prologue = self.n
        self.base, self.n = layer * self.per_layer + self.n, 0

    def leave_layers(self):
        assert self.n == self.per_layer, (self.n, self.per_layer)
        self.base, self.n = self.prologue + DEPTH * self.per_layer, 0

    def enter_loop(self, i, per_turn):
        self.saved = (self.base, self.n, per_turn)
        self.base = self.base + i * per_turn

    def leave_loop(self, turns):
        base, n, per_turn = self.saved
        assert self.n == n + per_turn, (self.n - n, per_turn)
        self.base, self.n = base, n + per_turn * turns


def build(nc, x_d, c_d, w_ada, b_ada, norm_pre, norm_post, w_ffn_in, w_ffn_out, w_in, b_forget, pool_w, pool_scale,
          conv_w, conv_b, dt_bias, a_log, d_skip, ssm_norm, w_ret_out, w_pool_out, w_ssm_out, w_fox_out, w_out,
          consts_d, out_d):
    with ExitStack() as ctx:
        ctx.enter_context(nc.allow_non_contiguous_dma(reason="small per-layer vectors"))
        cursor = [(nc.sbuf_base + 63) // 64 * 64]
        size_of = {F32: 4, F32R: 4}

        def at(name, shape, dt, offset):
            return nc.alloc_sbuf_tensor_at(name, shape, dt, offset=offset)

        def nbytes(shape):
            n = 4
            for s in shape[1:]:
                n *= s
            return (n + 31) // 32 * 32

        def sb(name, shape, dt=F32):
            off = cursor[0]
            cursor[0] += nbytes(shape)
            assert cursor[0] <= nc.sbuf_usable_end, (name, cursor[0])
            return at(name, shape, dt, off), off

        def sem(name):
            return ctx.enter_context(nc.semaphore(name))

        X, _ = sb("x_res", [P, KD, T])
        Y, y_off = sb("y_res", [P, KD, T])
        HH, _ = sb("h_hi", [P, KD, T], F32R)
        HL, hl_off = sb("h_lo", [P, KD, T], F32R)
        SQ = at("squares", [P, KD, T], F32, hl_off)
        H32 = at("h_full", [P, KD, T], F32, y_off)
        RAW, _ = sb("w_raw", [P, 4, 8 * COLS])
        WH, _ = sb("w_hi", [P, 4, 8 * P], F32R)
        WL, _ = sb("w_lo", [P, 4, 8 * P], F32R)
        KC, _ = sb("consts", [P, K_N])
        VECS, _ = sb("vectors", [P, DEPTH, V_N])
        VEC, _ = sb("vector", [P, V_N])
        ACC, _ = sb("ada_acc", [P, SUBS * D])
        SLAB, _ = sb("ada_slab", [P, 2, 2 * ADA_COLS])
        CS, _ = sb("c_silu", [P, KD])
        SILU1, _ = sb("silu_of_one", [P, 1])
        MODV, _ = sb("mod", [P, 24])
        AMOD, _ = sb("mod_scale", [P, 8])
        GMOD, _ = sb("mod_gate", [P, 8])
        RSTD, _ = sb("rstd", [P, 8])
        NV, _ = sb("newton_v", [P, 8])
        DG, _ = sb("diagonals", [P, TT, P])
        NT, _ = sb("newton_t", [P, 8])
        Z20, _ = sb("z20", [P, 2, 20])
        E20, _ = sb("e20", [P, 2, 20])
        S20, _ = sb("s20", [P, 2, 20])
        Q20, _ = sb("q20", [P, 2, 20])
        R20, _ = sb("r20", [P, 2, 20])
        DTV, _ = sb("dt", [P, 2, 16])
        DA, _ = sb("da", [P, 2, 20])
        AEXP, _ = sb("a_exp", [P, 20])
        ACUM, _ = sb("a_cum", [P, 2, 20])
        MX, _ = sb("fox_max", [P, 2, HEADS])
        SUM, _ = sb("fox_sum", [P, 2, HEADS])
        RIN, _ = sb("fox_rsum", [P, 2, HEADS])
        work = cursor[0]
        cursor_work = [work]

        def wk(name, shape, dt=F32):
            off = cursor_work[0]
            cursor_work[0] += nbytes(shape)
            assert cursor_work[0] <= nc.sbuf_usable_end, (name, cursor_work[0])
            return at(name, shape, dt, off), off

        AH, _ = wk("act_hi", [P, KF, T], F32R)
        AL, _ = wk("act_lo", [P, KF, T], F32R)
        GS, _ = wk("gate_silu", [P, 2, 2, T])
        A32, _ = wk("act_full", [P, 2, 2, T])
        cursor_work[0] = work
        SZ, _ = wk("z_silu", [P, 8, T])
        XBC, xbc_off = wk("xbc", [P, 12, T])
        XDT, xdt_off = wk("x_dt", [P, TT, D])
        YSH = at("y_ssm_hi", [P, 8, T], F32R, xbc_off)
        YSL = at("y_ssm_lo", [P, 8, T], F32R, xdt_off)
        FQ, fq_off = wk("fox_q", [P, HEADS, T])
        FK, fk_off = wk("fox_k", [P, HEADS, T])
        FV, _ = wk("fox_v", [P, TT, HEADS * P])
        YFH = at("y_fox_hi", [P, HEADS, T], F32R, fq_off)
        YFL = at("y_fox_lo", [P, HEADS, T], F32R, fk_off)
        PU, pu_off = wk("pool_u", [P, HEADS, T])
        PW, pw_off = wk("pool_w1", [P, HEADS, T])
        YPH = at("y_pool_hi", [P, HEADS, T], F32R, pu_off)
        YPL = at("y_pool_lo", [P, HEADS, T], F32R, pw_off)
        RV = at("ret_v", [P, TT, HEADS * P], F32, pu_off)
        RG = at("ret_g", [P, HEADS, T], F32, pw_off)
        RQ, rq_off = wk("ret_q", [P, HEADS, T])
        RK, rk_off = wk("ret_k", [P, HEADS, T])
        YRH = at("y_ret_hi", [P, HEADS, T], F32R, rq_off)
        YRL = at("y_ret_lo", [P, HEADS, T], F32R, rk_off)
        GATE, gate_off = wk("gate", [P, 2, T])
        SWAP = at("rotary_swap", [P, 2, T], F32, gate_off)
        SCR, scr_off = wk("scratch", [P, 2, HEADS, 384])
        SQM = at("squares_mix", [P, KD, T], F32, scr_off)
        SCF = [at(f"scratch_t{b}", [P, HEADS, T], F32, scr_off + b * HEADS * 384 * 4) for b in range(2)]
        SQS = at("squares_ssd", [P, 8, T], F32, xdt_off)
        CB = at("c_b_products", [P, 2, 384], F32, rk_off)
        PSLAB = at("ada_slab_first", [P, 8, 2 * ADA_COLS], F32, work)
        PM = at("pool_m", [P, P * HEADS], F32, rq_off)

        PS = ctx.enter_context(nc.psum_tensor("ps", [P, 8, 512], F32))

        def quad(b):
            return PS[:, b:b + 2, :].rearrange("p b (h i) -> p (b h) i", h=2)

        def con(a, n):
            return KC[:, a:a + n]

        ident = con(K_ID, P)
        one = con(K_ONE, 1)

        landed = [Signal(sem(f"unit_landed{s}"), UNITS // 4 * 16) for s in range(4)]
        w_hi = Signal(sem("w_hi_split"), 2 * UNITS)
        w_lo = Signal(sem("w_lo_split"), 2 * UNITS, before=8)
        w_used = Signal(sem("w_tile_used"), 2 * UNITS, before=4)
        bank_free = [Signal(sem(f"bank_pair_free{s}"), OUTS, before=1) for s in range(2)]
        ada_landed = [Signal(sem(f"ada_landed{s}"), SUBS * ADA_STEPS // 2 * 16) for s in range(2)]
        first_landed = [sem(f"ada_first_landed{s}") for s in range(8)]
        ada_used = Signal(sem("ada_used"), SUBS * ADA_STEPS, before=ADA_STEPS + 2)
        mod_ps = Signal(sem("mod_in_psum"), SUBS)
        modg_ps = Signal(sem("mod_gate_in_psum"), SUBS)
        mod_ok = Signal(sem("mod_ready"), SUBS)
        gmod_ok = Signal(sem("mod_gate_ready"), SUBS)
        xa_ok = Signal(sem("x_scaled_ready"), SUBS * 4)
        x_ready = Signal(sem("x_chunk_ready"), SUBS * 4)
        pre_sq = Signal(sem("pre_squared"), SUBS * 4)
        post_sq = Signal(sem("post_squared"), SUBS * 4)
        stat_ps = Signal(sem("stat_in_psum"), 8)
        rstd_ok = Signal(sem("rstd_ready"), 8)
        rb_ps = Signal(sem("rstd_rows_in_psum"), 8)
        h32_ok = Signal(sem("h_full_ready"), 12)
        hh_ok = Signal(sem("h_hi_ready"), 12)
        hl_ok = Signal(sem("h_lo_ready"), 12)
        mh_ok = Signal(sem("merged_hi_ready"), 4)
        ml_ok = Signal(sem("merged_lo_ready"), 4)
        sqsum_ok = Signal(sem("post_squares_summed"), SUBS)
        cb_ps = Signal(sem("c_b_in_psum"), 1)
        cb_ok = Signal(sem("c_b_ready"), 1)
        ydx_ok = Signal(sem("ssd_skip_added"), 4)
        rcos_ok = Signal(sem("rotary_cos_ready"), 4)
        gmul_ok = Signal(sem("gate_multiplied"), 12)
        y_ok = Signal(sem("y_evacuated"), SUBS * 4)
        gs_ok = Signal(sem("gate_silu_ready"), 2 * IN_PAIRS)
        a32_ok = Signal(sem("act_full_ready"), 2 * IN_PAIRS, before=2)
        ah_ok = Signal(sem("act_hi_ready"), 2 * IN_PAIRS)
        al_ok = Signal(sem("act_lo_ready"), 2 * IN_PAIRS, before=2)
        pu_ok = Signal(sem("pool_u_ready"), 2)
        pwin_ok = Signal(sem("pool_windows_ready"), 1)
        pooled_ok = Signal(sem("pooled_ready"), 1)
        pmix_ps = Signal(sem("pool_mixed_in_psum"), 1)
        yp32_ok = Signal(sem("y_pool_full_ready"), 1)
        yph_ok = Signal(sem("y_pool_hi_ready"), 1)
        ypl_ok = Signal(sem("y_pool_lo_ready"), 1)
        pm_ok = Signal(sem("pool_weights_landed"), 16)
        z_ok = Signal(sem("z_abs_ready"), 1)
        aexp_ok = Signal(sem("a_exp_ready"), 1)
        e_ok = Signal(sem("exp_abs_ready"), 1)
        da_ok = Signal(sem("da_ready"), 1)
        acum_ps = Signal(sem("a_cum_in_psum"), 1)
        acum_ok = Signal(sem("a_cum_ready"), 1)
        tap0_ok = Signal(sem("conv_tap0_ready"), 6)
        conv_ok = Signal(sem("conv_ready"), 6)
        xbc_ok = Signal(sem("xbc_silu_ready"), 6)
        fqkv_ok = Signal(sem("fox_qkv_ready"), 6)
        sz_ok = Signal(sem("z_silu_ready"), 4)
        xst_ps = Signal(sem("x_token_major_in_psum"), 1)
        xdt_ok = Signal(sem("x_dt_ready"), 1)
        ab_ps = Signal(sem("decay_rows_in_psum"), 4)
        seg_ok = Signal(sem("segments_ready"), 4)
        lm_ok = Signal(sem("decays_ready"), 4)
        m_ok = Signal(sem("masked_products_ready"), 4)
        yq_ps = Signal(sem("ssd_out_in_psum"), 4)
        ys_ok = Signal(sem("ssd_out_ready"), 4)
        ssm_sq = Signal(sem("ssd_squared"), 1)
        ys32_ok = Signal(sem("y_ssm_full_ready"), 4)
        ysh_ok = Signal(sem("y_ssm_hi_ready"), 4)
        ysl_ok = Signal(sem("y_ssm_lo_ready"), 1)
        fab_ps = Signal(sem("fox_decay_rows_in_psum"), 1)
        fx_ok = Signal(sem("fox_bias_ready"), 1)
        fs_ps = Signal(sem("fox_scores_in_psum"), 1)
        fmx_ok = Signal(sem("fox_max_ready"), 1)
        fp_ok = Signal(sem("fox_probs_ready"), 1)
        fpn_ok = Signal(sem("fox_probs_normalised"), 1)
        fpt_ps = Signal(sem("fox_probs_transposed"), 1)
        fpt_ok = Signal(sem("fox_probs_t_ready"), 1)
        fo_ps = Signal(sem("fox_out_in_psum"), 1)
        yfh_ok = Signal(sem("y_fox_hi_ready"), 1)
        yfl_ok = Signal(sem("y_fox_lo_ready"), 1)
        swap_ok = Signal(sem("rotary_swapped"), 4)
        rot_ok = Signal(sem("rotary_ready"), 4)
        rvg_ok = Signal(sem("ret_vg_ready"), 4)
        rs_ps = Signal(sem("ret_scores_in_psum"), 1)
        rs_ok = Signal(sem("ret_scores_ready"), 1)
        ro_ps = Signal(sem("ret_out_in_psum"), 1)
        ro_ok = Signal(sem("ret_out_ready"), 1)
        rm_ps = Signal(sem("ret_mean_in_psum"), 1)
        rc_ok = Signal(sem("ret_centred"), 1)
        rsq_ok = Signal(sem("ret_squared"), 1)
        yr32_ok = Signal(sem("y_ret_full_ready"), 1)
        yrh_ok = Signal(sem("y_ret_hi_ready"), 1)
        yrl_ok = Signal(sem("y_ret_lo_ready"), 1)
        gate_ok = Signal(sem("gate_ready"), 16)
        gated_ok = Signal(sem("gate_used"), 16, before=1)
        loaded = sem("small_inputs_landed")
        x_landed = sem("x_landed")
        dec_landed = sem("retention_decays_landed")
        c_landed = sem("c_landed")
        passed = sem("waits_passed")
        c_ok = sem("c_silu_ready")
        turned = sem("inputs_transposed")
        vecs_ok = sem("vectors_ready")
        zero_bank = sem("vector_banks_read")
        fin_ps = sem("result_in_psum")
        fin_ok = sem("result_ready")
        stored = sem("result_stored")
        dve_chain = sem("dve_chain")
        act_chain = sem("act_chain")
        pool_chain = sem("pool_chain")

        ST_PRE, ST_POST, ST_SSM, ST_RET = (0, 2, 6), (1, 5, 7), 3, 4
        H_PRE = (0, 4, 8)
        N_LOADS = 1 + DEPTH * 12
        VROWS = [at(f"vector_rows{b}", [P, DEPTH, P], F32, hl_off + b * DEPTH * P * 4) for b in range(2)]
        XTOK = at("x_tokens", [P, TT, D], F32, y_off)

        block = ctx.enter_context(nc.Block())

        @block.sync
        def _(sp):
            sp.dma_start(CS[:], c_d.rearrange("a (k p) -> p (a k)", p=P)).then_inc(c_landed, 16)

            def unit(layer, u, i, kn, cols, src, step=0):
                s = u % 4
                sp.wait_ge(w_lo.sem, w_lo.at(layer, 2 * (u - 4) + 2 + i * (2 * step)))
                sp.sem_inc(passed, 1)
                sp.dma_start(RAW[:, s, 0:kn * cols].rearrange("p (k n) -> p k n", k=kn),
                             src.rearrange("(k p) n -> p k n", p=P)).then_inc(landed[s].sem, 16)

            def first_in_unit(layer, u, r, src_layer):
                unit(layer, u, 0, KD, COLS, w_ffn_in[src_layer, 0, :, r * FF:r * FF + COLS])

            def first_slab(e, piece):
                src = w_ada[0, (e % 4) * 2 * P:(e % 4 + 1) * 2 * P, piece * ADA_COLS:(piece + 1) * ADA_COLS]
                sp.dma_start(PSLAB[:, e, :].rearrange("p (k n) -> p k n", k=2),
                             src.rearrange("(k p) n -> p k n", p=P)).then_inc(first_landed[e], 16)

            for r in range(2):
                first_in_unit(0, r, r, 0)
            sp.dma_start(KC[:, 0:K_DEC], consts_d[:, 0:K_DEC]).then_inc(loaded, 16)
            sp.dma_start(XTOK[:], x_d.rearrange("a (t p) d -> p (a t) d", p=P)).then_inc(x_landed, 16)
            for l in range(DEPTH):
                for rows, dst, src in (
                    (72, VROWS[0][0:72, l, :], b_ada[l, :].rearrange("(r q) -> r q", q=P)),
                    (48, VROWS[0][72:96, l, :], norm_pre[l].rearrange("s (r q) -> (s r) q", q=P)),
                    (48, VROWS[0][96:120, l, :], norm_post[l].rearrange("s (r q) -> (s r) q", q=P)),
                    (8, VROWS[1][0:8, l, :], ssm_norm[l, :].rearrange("(r q) -> r q", q=P)),
                    (4, VROWS[1][8:12, l, :], pool_scale[l, :].rearrange("(r q) -> r q", q=P)),
                    (12, VROWS[1][12:24, l, :], conv_b[l, :].rearrange("(r q) -> r q", q=P)),
                    (48, VROWS[1][24:72, l, :], conv_w[l].rearrange("s (r q) -> (s r) q", q=P)),
                    (0, VECS[:, l, V_B20:V_B20 + 16], dt_bias[l, :].partition_broadcast(P)),
                    (0, VECS[:, l, V_B20 + 16:V_B20 + 20], b_forget[l, :].partition_broadcast(P)),
                    (0, VECS[:, l, V_ALOG:V_ALOG + 16], a_log[l, :].partition_broadcast(P)),
                    (0, VECS[0:64, l, V_DSK:V_DSK + 8], d_skip[l, 0:16:2].partition_broadcast(64)),
                    (0, VECS[64:128, l, V_DSK:V_DSK + 8], d_skip[l, 1:16:2].partition_broadcast(64)),
                ):
                    sp.dma_start(dst, src).then_inc(loaded, 16)

            def ada_slab(layer, sub, piece, r, ring):
                src = w_ada[layer, r * 2 * P:(r + 1) * 2 * P, bass.ds(sub * SUBS * D + piece * ADA_COLS, ADA_COLS)]
                sp.dma_start(SLAB[:, ring, :].rearrange("p (k n) -> p k n", k=2),
                             src.rearrange("(k p) n -> p k n", p=P)).then_inc(ada_landed[ring].sem, 16)

            for e in range(8):
                first_slab(e, e // 4)
            for e in range(8):
                sp.wait_ge(ada_used.sem, 2 + e + 1)
                first_slab(e, 2 + e // 4)
            sp.dma_start(KC[:, K_DEC:K_N], consts_d[:, K_DEC:K_N]).then_inc(dec_landed, 16)

            def ada_next(layer, sub, piece, r):
                n = sub * ADA_STEPS + r
                sp.wait_ge(ada_used.sem, ada_used.at(layer, n - 1 + piece * 4))
                sp.sem_inc(passed, 1)
                if sub < 2:
                    ada_slab(layer, sub + 1, piece, r, r % 2)
                else:
                    ada_slab((DEPTH - 1) - layer, 0, piece, r, r % 2)

            def ffn(layer, f):
                ub, sub = UB_FFN[f], 2 * f

                def in_unit(i, r):
                    src = w_ffn_in[layer, f, :, bass.ds((r % 2) * FF + (r // 2) * COLS + i * (2 * COLS), COLS)]
                    unit(layer, ub + r, i, KD, COLS, src, step=4)

                for r in range(0 if f else 2, 4):
                    in_unit(0, r)
                with sp.Fori(1, 5) as i:
                    for r in range(4):
                        in_unit(i, r)
                        ada_next(layer, sub, i - 1, r)
                for r in (20, 21):
                    src = w_ffn_in[layer, f, :, (r % 2) * FF + (r // 2) * COLS:(r % 2) * FF + (r // 2) * COLS + COLS]
                    unit(layer, ub + r, 0, KD, COLS, src)
                for p in range(4):
                    for q in range(4):
                        rows = slice(OUT_START[q] * P, (OUT_START[q] + OUT_SPLIT[q]) * P)
                        unit(layer, ub + 22 + 4 * p + q, 0, OUT_SPLIT[q], COLS,
                             w_ffn_out[layer, f, rows, p * COLS:(p + 1) * COLS])

            with sp.Fori(0, DEPTH) as layer:
                ffn(layer, 0)
                for u, (what, col, kn, cols) in enumerate(MIX):
                    w = {"ret": w_ret_out, "pool": w_pool_out, "ssm": w_ssm_out, "fox": w_fox_out,
                         "wout": w_out}.get(what, w_in)
                    unit(layer, UB_MIX + u, 0, kn, cols, w[layer, :, col:col + cols])
                    if u == 4:
                        sp.wait_ge(pu_ok.sem, pu_ok.at(layer, 1))
                        sp.sem_inc(passed, 1)
                        sp.dma_start(PM[:].rearrange("c (g d) -> c g d", g=HEADS),
                                     pool_w[layer].rearrange("g c d -> c g d")).then_inc(pm_ok.sem, 16)
                    for n in range(ADA_STEPS):
                        if u == (ADA_AT[n - 2] + 6 if n >= 2 else 6 + n):
                            ada_next(layer, 1, n // 4, n % 4)
                ffn(layer, 1)
                for r in range(2):
                    first_in_unit(layer, UNITS + r, r, (DEPTH - 1) - layer)
            sp.wait_ge(fin_ok, 1)
            sp.dma_start(out_d.rearrange("a (t p) d -> p (a t) d", p=P), XTOK[:]).then_inc(stored, 16)
            sp.wait_ge(stored, 16)

        @block.tensor
        def _(pe):
            mm = pe.matmul

            def dense_unit(layer, u, kn, k0, hi, lo, pair, first=True, last=True, i=0, step=0, merged=False):
                for t in range(2):
                    m = 2 * u + t
                    pe.wait_ge(w_lo.sem, w_lo.at(layer, m + 1 + i * (2 * step)))
                    slot = m % 4
                    out = PS[:, 2 * pair + t, 0:T]
                    for k in range(kn):
                        c = slice(k * P, (k + 1) * P)
                        a = k0 + k
                        if merged and t == 0 and k % 2 == 0:
                            pe.wait_ge(ml_ok.sem, ml_ok.at(layer, k // 2 + 1))
                        mm(out, WH[:, slot, c], hi[:, a, :], start=first and k == 0, stop=False)
                        mm(out, WH[:, slot, c], lo[:, a, :], start=False, stop=False)
                        ins = mm(out, WL[:, slot, c], hi[:, a, :], start=False, stop=last and k == kn - 1)
                    ins.then_inc(w_used.sem, 1)

            def first_units(layer, u, n0):
                for pair in range(2):
                    pe.wait_ge(w_lo.sem, w_lo.at(layer, 2 * u + 2 * pair + 2))
                for c in range(4):
                    pe.wait_ge(hh_ok.sem, hh_ok.at(layer, n0 + c + 1))
                    for tile in range(4):
                        slot = (2 * u + tile) % 4
                        for k in (2 * c, 2 * c + 1):
                            cs = slice(k * P, (k + 1) * P)
                            mm(PS[:, tile, 0:T], WH[:, slot, cs], HH[:, k, :], start=(k == 0), stop=False)
                            mm(PS[:, tile, 0:T], WL[:, slot, cs], HH[:, k, :], start=False, stop=False)
                    pe.wait_ge(hl_ok.sem, hl_ok.at(layer, n0 + c + 1))
                    for tile in range(4):
                        slot = (2 * u + tile) % 4
                        for k in (2 * c, 2 * c + 1):
                            ins = mm(PS[:, tile, 0:T], WH[:, slot, k * P:(k + 1) * P], HL[:, k, :], start=False,
                                     stop=(k == KD - 1))
                        if c == 3:
                            ins.then_inc(w_used.sem, 1)

            def token_unit(layer, u, cols, pair):
                m = 2 * u
                pe.wait_ge(w_lo.sem, w_lo.at(layer, m + 2))
                s = m % 4
                for tt in range(TT):
                    tok = slice(tt * P, (tt + 1) * P)
                    out = PS[:, 2 * pair + tt, 0:cols]
                    for k in range(KD):
                        if cols == COLS:
                            wh, wl = WH[:, s:s + 2, k * P:(k + 1) * P], WL[:, s:s + 2, k * P:(k + 1) * P]
                            out = PS[:, 2 * pair + tt, 0:cols].rearrange("p (a b) -> p a b", a=2)
                        else:
                            wh, wl = WH[:, s, k * cols:(k + 1) * cols], WL[:, s, k * cols:(k + 1) * cols]
                        mm(out, HH[:, k, tok], wh, start=(k == 0), stop=False)
                        mm(out, HH[:, k, tok], wl, start=False, stop=False)
                        ins = mm(out, HL[:, k, tok], wh, start=False, stop=(k == KD - 1))
                ins.then_inc(w_used.sem, 2)

            def stat_tiles(sq, tiles, first, last):
                for k in tiles:
                    for tt in range(TT):
                        ins = mm(PS[:, 4 + tt, 0:1], sq[:, k, tt * P:(tt + 1) * P], one,
                                 start=(first and k == tiles[0]), stop=(last and k == tiles[-1]))
                return ins

            def stat_rows(sq, tiles, first, last):
                for k in tiles:
                    ins = mm(PS[:, 4, 0:T], con(K_MEAN, P), sq[:, k, :], start=(first and k == tiles[0]),
                             stop=(last and k == tiles[-1]))
                return ins

            def post_stat(layer, s, sq):
                pe.wait_ge(post_sq.sem, post_sq.at(layer, 4 * s + 4))
                stat_tiles(sq, (6, 7), False, True).then_inc(stat_ps.sem, 1)

            def post_stat_sum(layer, s, sq):
                pe.wait_ge(sqsum_ok.sem, sqsum_ok.at(layer, s + 1))
                stat_tiles(sq, (0, 1), True, False)

            def mod_sums(cols):
                for j in cols:
                    ins = mm(PS[:, 7 if j < 16 else 5, j:j + 1], ACC[:, j * P:(j + 1) * P], one, start=True, stop=True)
                if cols[-1] == 15:
                    ins.then_inc(mod_ps.sem, 1)
                if cols[-1] == 23:
                    ins.then_inc(modg_ps.sem, 1)

            def rstd_rows(layer, which, heads=1, bank=6):
                pe.wait_ge(rstd_ok.sem, rstd_ok.at(layer, which + 1))
                for h in range(heads):
                    for tt in range(TT):
                        col = (h * T + tt * P) % 512
                        ins = mm(PS[:, bank + h // 2, col:col + P],
                                 RSTD[:, tt * heads + h:tt * heads + h + 1].to_broadcast([P, P]), ident,
                                 start=True, stop=True)
                ins.then_inc(rb_ps.sem, 1)

            def keep_busy(n):
                for _ in range(n):
                    mm(PS[:, 0, 0:T], ident, con(K_COS, T), start=True, stop=True)

            def pre(layer, s):
                for c in range(4):
                    pe.wait_ge(pre_sq.sem, pre_sq.at(layer, 4 * s + c + 1))
                    ins = stat_rows(SQ, (2 * c, 2 * c + 1), c == 0, c == 3)
                    if c == 3:
                        ins.then_inc(stat_ps.sem, 1)
                    elif c < 2:
                        mod_sums(range(12 + 2 * c, 14 + 2 * c))
                pe.wait_ge(ada_used.sem, ada_used.at(layer, s * ADA_STEPS))
                for j in (16, 20):
                    mod_sums(range(j, j + 4))
                    keep_busy(KEEP[2])
                rstd_rows(layer, ST_PRE[s])
                keep_busy(KEEP[3])

            def post(layer, s, sq):
                post_stat(layer, s, sq)
                after = layer + (0 if s < 2 else 1)
                pe.wait_ge(bank_free[0].sem, bank_free[0].at(layer, OB_NEXT[s]))
                pe.wait_ge(ada_used.sem, ada_used.at(after, (s + 1) % SUBS * ADA_STEPS))
                keep_busy(KEEP[0])
                mod_sums(range(0, 6))
                rstd_rows(layer, ST_POST[s])
                keep_busy(KEEP[1])
                mod_sums(range(6, 12))

            def ffn(layer, f):
                s, ub, ob = 2 * f, UB_FFN[f], OB_FFN[f]
                pre(layer, s)
                for pair in range(2):
                    pe.wait_ge(bank_free[pair].sem, bank_free[pair].at(layer, ob))
                first_units(layer, ub, H_PRE[s])

                def in_unit(i, r):
                    pe.wait_ge(bank_free[r % 2].sem, bank_free[r % 2].at(layer, ob + r // 2 + i * 2))
                    dense_unit(layer, ub + r, KD, 0, HH, HL, r % 2, i=i, step=4)

                pe.sem_inc(passed, 1)
                with pe.Fori(0, 5) as i:
                    for r in (2, 3, 4, 5):
                        in_unit(i, r)
                for p in range(4):
                    pe.wait_ge(bank_free[p % 2].sem, bank_free[p % 2].at(layer, ob + IN_PAIRS + p // 2))
                    for q in range(4):
                        if p == 0:
                            pairs = (OUT_START[q] + OUT_SPLIT[q] + 1) // 2
                            pe.wait_ge(al_ok.sem, al_ok.at(layer, f * IN_PAIRS + pairs))
                        if p == 3 and q == 3:
                            post_stat_sum(layer, s, SQ)
                        dense_unit(layer, ub + 22 + 4 * p + q, OUT_SPLIT[q], OUT_START[q], AH, AL, p % 2,
                                   first=(q == 0), last=(q == 3))
                post(layer, s, SQ)

            def scores(q, k, h):
                mm(PS[:, 4 + h, 0:T], k[:, h, 0:P], q[:, h, :], start=True, stop=True)
                return mm(PS[:, 4 + h, T:384], k[:, h, P:T], q[:, h, P:T], start=True, stop=True)

            def weighted(v, s, h):
                out = quad(4)[:, h, :]
                mm(out, v[:, 0, h * P:(h + 1) * P], s[:, h, 0:T], start=True, stop=False)
                return mm(out[:, P:T], v[:, 1, h * P:(h + 1) * P], s[:, h, T:384], start=False, stop=True)

            def decay_rows(h, out):
                mm(out[:, 0:P], DA[:, 0, h:h + 1].to_broadcast([P, P]), con(K_T0, P), start=True, stop=True)
                return mm(out[:, P:T], DA[:, 1, h:h + 1].to_broadcast([P, P]), con(K_T1, P), start=True, stop=True)

            def mixer_core(layer, u):
                if u == 8:
                    pe.wait_ge(da_ok.sem, da_ok.at(layer, 1))
                    mm(PS[:, 4, 0:20], con(K_T0, P), DA[:, 0, :], start=True, stop=True)
                    mm(PS[:, 5, 0:20], con(K_T1, P), DA[:, 1, :], start=True, stop=True).then_inc(acum_ps.sem, 1)
                if u == 12:
                    pe.wait_ge(acum_ok.sem, acum_ok.at(layer, 1))
                    pe.wait_ge(xbc_ok.sem, xbc_ok.at(layer, 6))
                    for k in range(8):
                        for tt in range(TT):
                            col = tt * D + k * P
                            ins = pe.transpose(PS[:, 4 + col // 512, col % 512:col % 512 + P],
                                               XBC[:, k, tt * P:(tt + 1) * P], ident)
                    ins.then_inc(xst_ps.sem, 1)
                if u == 14:
                    pe.wait_ge(xdt_ok.sem, xdt_ok.at(layer, 1))
                    for g in range(2):
                        mm(PS[:, 6 + g, 0:T], XBC[:, 8 + g, 0:P], XBC[:, 10 + g, :], start=True, stop=True)
                        ins = mm(PS[:, 6 + g, T:384], XBC[:, 8 + g, P:T], XBC[:, 10 + g, P:T], start=True, stop=True)
                    ins.then_inc(cb_ps.sem, 1)
                    pe.wait_ge(pm_ok.sem, pm_ok.at(layer, 16))
                    pe.wait_ge(pooled_ok.sem, pooled_ok.at(layer, 1))
                    for g in range(HEADS):
                        src = PW if g % 2 == 0 else SCF[1]
                        ins = mm(quad(4)[:, g, :], PM[:, g * P:(g + 1) * P], src[:, g, :], start=True, stop=True)
                    ins.then_inc(pmix_ps.sem, 1)
                for q in range(4):
                    if u == 20 + 2 * q:
                        pe.wait_ge(m_ok.sem, m_ok.at(layer, q + 1))
                        if q:
                            pe.wait_ge(ydx_ok.sem, ydx_ok.at(layer, q))
                        else:
                            pe.wait_ge(cb_ok.sem, cb_ok.at(layer, 1))
                        for j in range(2):
                            for e in range(2):
                                h4 = 2 * j + e
                                h = 4 * q + h4
                                rows = slice(64 * e, 64 * e + 64)
                                out = PS[rows, 7, j * T:(j + 1) * T]
                                mm(out, XDT[:, 0, h * SHD:(h + 1) * SHD], SCR[:, q % 2, h4, 0:T], start=True, stop=False)
                                ins = mm(PS[rows, 7, j * T + P:(j + 1) * T], XDT[:, 1, h * SHD:(h + 1) * SHD],
                                         SCR[:, q % 2, h4, T:384], start=False, stop=True)
                        ins.then_inc(yq_ps.sem, 1)
                for q in range(4):
                    if u == 16 + 2 * q:
                        if q == 0:
                            pe.wait_ge(yp32_ok.sem, yp32_ok.at(layer, 1))
                        else:
                            pe.wait_ge(seg_ok.sem, seg_ok.at(layer, q))
                        for h4 in range(4):
                            ins = decay_rows(4 * q + h4, quad(4)[:, h4, :])
                        ins.then_inc(ab_ps.sem, 1)
                if u == 24:
                    pe.wait_ge(seg_ok.sem, seg_ok.at(layer, 4))
                    for h in range(HEADS):
                        ins = decay_rows(16 + h, quad(4)[:, h, :])
                    ins.then_inc(fab_ps.sem, 1)
                if u == 29:
                    pe.wait_ge(fx_ok.sem, fx_ok.at(layer, 1))
                    pe.wait_ge(ydx_ok.sem, ydx_ok.at(layer, 4))
                    pe.wait_ge(fqkv_ok.sem, fqkv_ok.at(layer, 4))
                    for h in range(HEADS):
                        mm(PS[:, 4 + h, 0:P], FQ[:, h, 0:P], FK[:, h, 0:P], start=True, stop=True)
                        ins = mm(PS[:, 4 + h, P:384], FQ[:, h, P:T], FK[:, h, :], start=True, stop=True)
                    ins.then_inc(fs_ps.sem, 1)
                if u == 31:
                    pe.wait_ge(fmx_ok.sem, fmx_ok.at(layer, 1))
                    pe.wait_ge(ssm_sq.sem, ssm_sq.at(layer, 1))
                    stat_rows(SQS, range(8), True, True).then_inc(stat_ps.sem, 1)
                if u == 33:
                    rstd_rows(layer, ST_SSM)
                if u == 36:
                    pe.wait_ge(ys32_ok.sem, ys32_ok.at(layer, 4))
                    pe.wait_ge(fpn_ok.sem, fpn_ok.at(layer, 1))
                    for h in range(HEADS):
                        pe.transpose(PS[:, 4 + h, 0:P], SCR[:, 1, h, 0:P], ident)
                        pe.transpose(PS[:, 4 + h, P:T], SCR[:, 1, h, P:T], ident)
                        ins = pe.transpose(PS[:, 4 + h, T:384], SCR[:, 1, h, T:384], ident)
                    ins.then_inc(fpt_ps.sem, 1)
                if u == 37:
                    pe.wait_ge(fpt_ok.sem, fpt_ok.at(layer, 1))
                    pe.wait_ge(fqkv_ok.sem, fqkv_ok.at(layer, 6))
                    for h in range(HEADS):
                        ins = weighted(FV, SCR[:, 0], h)
                    ins.then_inc(fo_ps.sem, 1)
                if u == 40:
                    pe.wait_ge(rot_ok.sem, rot_ok.at(layer, 4))
                    pe.wait_ge(yfl_ok.sem, yfl_ok.at(layer, 1))
                    for h in range(HEADS):
                        ins = scores(RQ, RK, h)
                    ins.then_inc(rs_ps.sem, 1)
                if u == 42:
                    pe.wait_ge(rs_ok.sem, rs_ok.at(layer, 1))
                    pe.wait_ge(rvg_ok.sem, rvg_ok.at(layer, 2))
                    for h in range(HEADS):
                        ins = weighted(RV, SCR[:, 1], h)
                    ins.then_inc(ro_ps.sem, 1)
                if u == 44:
                    pe.wait_ge(ro_ok.sem, ro_ok.at(layer, 1))
                    for b in range(2):
                        ins = mm(PS[:, 6 + b, :], con(K_MEAN, P), SCF[0][:, 2 * b:2 * b + 2, :], start=True, stop=True)
                    ins.then_inc(rm_ps.sem, 1)
                if u == 47:
                    pe.wait_ge(rsq_ok.sem, rsq_ok.at(layer, 1))
                    for tt in range(TT):
                        for h in range(HEADS):
                            ins = mm(PS[:, 4 + tt, h:h + 1], SCF[1][:, h, tt * P:(tt + 1) * P], one, start=True, stop=True)
                    ins.then_inc(stat_ps.sem, 1)
                if u == 50:
                    rstd_rows(layer, ST_RET, heads=HEADS, bank=4)

            def mixer(layer):
                pre(layer, 1)
                acts = {"ret": (YRH, YRL, yrl_ok, 1), "pool": (YPH, YPL, ypl_ok, 1),
                        "ssm": (YSH, YSL, ysl_ok, 1), "fox": (YFH, YFL, yfl_ok, 1)}
                for u, (what, col, kn, cols) in enumerate(MIX):
                    mixer_core(layer, u)
                    pair = u % 2
                    pe.wait_ge(bank_free[pair].sem, bank_free[pair].at(layer, OB_MIX + u // 2))
                    if u == 0:
                        continue
                    if u == 1:
                        first_units(layer, UB_MIX, H_PRE[1])
                        continue
                    if what in FEATURE_ROWS:
                        token_unit(layer, UB_MIX + u, cols, pair)
                        continue
                    hi, lo = (YSH, YSL) if what == "wout" else (HH, HL)
                    if what in acts:
                        hi, lo, ready, n = acts[what]
                        if col == 0:
                            pe.wait_ge(ready.sem, ready.at(layer, n))
                    dense_unit(layer, UB_MIX + u, kn, 0, hi, lo, pair, merged=(u == 60))
                post_stat_sum(layer, 1, SQM)
                post(layer, 1, SQM)

            pe.wait_ge(x_landed, 16)
            pe.wait_ge(loaded, 16 * N_LOADS)
            for k in range(KD):
                for tt in range(TT):
                    col = (k % 2) * T + tt * P
                    ins = pe.transpose(PS[:, 4 + k // 2, col:col + P], XTOK[:, tt, k * P:(k + 1) * P], ident)
            ins.then_inc(turned, 1)
            for l in range(DEPTH):
                pe.transpose(PS[:, l, 0:120], VROWS[0][0:120, l, :], KC[0:120, K_ID:K_ID + 120])
                ins = pe.transpose(PS[:, l, 120:192], VROWS[1][0:72, l, :], KC[0:72, K_ID:K_ID + 72])
            ins.then_inc(turned, 1)
            pe.wait_ge(zero_bank, 1)
            pe.wait_ge(ada_used.sem, 2 + ADA_STEPS // 2)
            mod_sums(range(0, 12))
            pe.wait_ge(ada_used.sem, 2 + ADA_STEPS // 4 * 3)
            with pe.Fori(0, DEPTH) as layer:
                ffn(layer, 0)
                mixer(layer)
                ffn(layer, 1)
            pe.wait_ge(x_ready.sem, 4 + DEPTH * SUBS * 4)
            for k in range(KD):
                for tt in range(TT):
                    col = tt * D + k * P
                    ins = pe.transpose(PS[:, 4 + col // 512, col % 512:col % 512 + P], X[:, k, tt * P:(tt + 1) * P], ident)
            ins.then_inc(fin_ps, 1)

        @block.scalar
        def _(act):
            fn = act.activation

            def split(layer, u, kn, cols=COLS, i=0, step=0):
                s = u % 4
                act.wait_ge(landed[s].sem, landed[s].at(layer, (u // 4 + 1) * 16 + i * (16 * (step // 4))))
                for t in range(2 if cols == COLS else 1):
                    m = 2 * u + t
                    act.wait_ge(w_used.sem, w_used.at(layer, m - 3 + i * (2 * step)))
                    n = P if cols == COLS else cols
                    raw = RAW[:, s, 0:kn * cols].rearrange("p (k n) -> p k n", k=kn)[:, :, t * n:(t + 1) * n]
                    fn(WH[:, m % 4, 0:kn * n].rearrange("p (k n) -> p k n", k=kn), raw, ACT.Copy)\
                        .then_inc(w_hi.sem, 1 if cols == COLS else 2)

            def done(layer, u, i=0, step=0):
                act.wait_ge(w_used.sem, w_used.at(layer, 2 * u + 2 + i * (2 * step)))

            def pre(layer, s):
                for c in range(4):
                    act.wait_ge(x_ready.sem, x_ready.at(layer, 4 * s + c + 1))
                    fn(SQ[:, 2 * c:2 * c + 2, :], X[:, 2 * c:2 * c + 2, :], ACT.Square).then_inc(pre_sq.sem, 1)
                act.wait_ge(mod_ok.sem, mod_ok.at(layer, s + 1))
                for c in range(4):
                    for k in (2 * c, 2 * c + 1):
                        ins = fn(H32[:, k, :], X[:, k, :], ACT.Identity, scale=AMOD[:, k:k + 1])
                    ins.then_inc(xa_ok.sem, 1)
                for c in range(4):
                    act.wait_ge(h32_ok.sem, h32_ok.at(layer, H_PRE[s] + c + 1))
                    for k in (2 * c, 2 * c + 1):
                        ins = fn(HH[:, k, :], H32[:, k, :], ACT.Identity, bias=MODV[:, k:k + 1])
                    ins.then_inc(hh_ok.sem, 1)

            def merged_hi(layer, c):
                act.wait_ge(gated_ok.sem, gated_ok.at(layer, 12 + c + 1))
                fn(YSH[:, 2 * c:2 * c + 2, :], Y[:, 2 * c:2 * c + 2, :], ACT.Copy).then_inc(mh_ok.sem, 1)

            def y_out(layer, s, p, pair, u, sq):
                if p == 0:
                    act.wait_ge(gmod_ok.sem, gmod_ok.at(layer, s + 1))
                done(layer, u)
                src = PS[:, 2 * pair:2 * pair + 2, 0:T]
                fn(sq[:, 2 * p:2 * p + 2, :], src, ACT.Square).then_inc(post_sq.sem, 1)
                for t in range(2):
                    k = 2 * p + t
                    ins = fn(Y[:, k, :], PS[:, 2 * pair + t, 0:T], ACT.Identity, scale=GMOD[:, k:k + 1])
                ins.then_inc(y_ok.sem, 1)
                act.wait_ge(y_ok.sem, y_ok.at(layer, 4 * s + p + 1))
                act.sem_inc(bank_free[pair].sem, 1)

            def ffn(layer, f):
                ub, s = UB_FFN[f], 2 * f
                fn(SILU1[:], one, ACT.Silu)
                pre(layer, s)

                def gate_unit(i, r, kn_next):
                    split(layer, ub + r + 2, kn_next, i=i, step=4)
                    done(layer, ub + r, i, 4)
                    j = f * IN_PAIRS + r // 2
                    act.wait_ge(a32_ok.sem, a32_ok.at(layer, j - 1 + i * 2))
                    fn(GS[:, (r // 2) % 2, :, :], PS[:, 0:2, 0:T], ACT.Silu).then_inc(gs_ok.sem, 1)
                    act.wait_ge(gs_ok.sem, gs_ok.at(layer, i * 2 + (j + 1)))
                    act.sem_inc(bank_free[0].sem, 1)

                def up_unit(i, r, kn_next):
                    split(layer, ub + r + 2, kn_next, i=i, step=4)
                    j = f * IN_PAIRS + r // 2
                    act.wait_ge(a32_ok.sem, a32_ok.at(layer, j + 1 + i * 2))
                    fn(AH[:, bass.ds(i * 4 + (r // 2) * 2, 2), :], A32[:, (r // 2) % 2, :, :], ACT.Copy)\
                        .then_inc(ah_ok.sem, 1)

                with act.Fori(0, 5) as i:
                    for r in (0, 2):
                        gate_unit(i, r, KD)
                        up_unit(i, r + 1, KD)
                gate_unit(0, 20, OUT_SPLIT[0])
                up_unit(0, 21, OUT_SPLIT[1])
                for r in range(22, FFN_UNITS):
                    if r + 2 < FFN_UNITS:
                        split(layer, ub + r + 2, OUT_SPLIT[(r - 20) % 4])
                    else:
                        split(layer, ub + r + 2, KD)
                    if r % 4 == 1:
                        p = (r - 22) // 4
                        y_out(layer, s, p, p % 2, ub + r, SQ)

            def mixer(layer):
                pre(layer, 1)
                for u, (what, col, kn, cols) in enumerate(MIX):
                    g = UB_MIX + u
                    pair = u % 2
                    src = PS[:, 2 * pair:2 * pair + 2, 0:T]
                    if u == 60:
                        merged_hi(layer, 3)
                    if u + 2 < MIX_UNITS:
                        split(layer, g + 2, MIX[u + 2][2], MIX[u + 2][3])
                    else:
                        split(layer, g + 2, KD)
                    if what in ("pu", "fq", "fk"):
                        done(layer, g)
                        dst, c0, sig = {"pu": (PU, C_PU, pu_ok), "fq": (FQ, C_FQ, fqkv_ok), "fk": (FK, C_FK, fqkv_ok)}[what]
                        t = (col - c0) // P
                        fn(dst[:, t:t + 2, :], src, ACT.Copy).then_inc(sig.sem, 1)
                        act.wait_ge(sig.sem, sig.at(layer, u - (0 if what == "pu" else 10) + 1))
                        act.sem_inc(bank_free[pair].sem, 1)
                    if what in ("fv", "rv"):
                        done(layer, g)
                        dst, c0, sig, n = {"fv": (FV, C_FV, fqkv_ok, u - 9), "rv": (RV, C_RV, rvg_ok, u - 31)}[what]
                        fn(dst[:, :, col - c0:col - c0 + COLS], src, ACT.Copy).then_inc(sig.sem, 1)
                        act.wait_ge(sig.sem, sig.at(layer, n))
                        act.sem_inc(bank_free[pair].sem, 1)
                    if what == "rg":
                        done(layer, g)
                        t = (col - C_RG) // P
                        fn(RG[:, t:t + 2, :], src, ACT.Silu).then_inc(rvg_ok.sem, 1)
                        act.wait_ge(rvg_ok.sem, rvg_ok.at(layer, u - 31))
                        act.sem_inc(bank_free[pair].sem, 1)
                    if what == "sz":
                        done(layer, g)
                        t = (col - C_SZ) // P
                        fn(SZ[:, t:t + 2, :], src, ACT.Silu).then_inc(sz_ok.sem, 1)
                        act.wait_ge(sz_ok.sem, sz_ok.at(layer, u - 15))
                        act.sem_inc(bank_free[pair].sem, 1)
                    if what == "xbc":
                        done(layer, g)
                        t0 = (col - C_XBC) // P
                        for t in range(2):
                            w3 = VEC[:, V_CW + 36 + t0 + t:V_CW + 36 + t0 + t + 1]
                            b = VEC[:, V_CB + t0 + t:V_CB + t0 + t + 1]
                            ins = fn(XBC[:, t0 + t, :], PS[:, 2 * pair + t, 0:T], ACT.Identity, scale=w3, bias=b)
                        ins.then_inc(tap0_ok.sem, 1)
                    if what in ("rq", "rk"):
                        done(layer, g)
                        n = u - 28
                        if n == 0:
                            act.wait_ge(gated_ok.sem, gated_ok.at(layer, 4))
                        else:
                            act.wait_ge(rot_ok.sem, rot_ok.at(layer, n))
                        fn(SWAP[0:64, :, :], PS[64:128, 2 * pair:2 * pair + 2, 0:T], ACT.Copy)
                        fn(SWAP[64:128, :, :], PS[0:64, 2 * pair:2 * pair + 2, 0:T], ACT.Copy).then_inc(swap_ok.sem, 1)
                    if what == "gate":
                        done(layer, g)
                        n = (u - 20) // 2 if u < 28 else 4 + (u - 36) // 2
                        if n == 4:
                            act.wait_ge(rot_ok.sem, rot_ok.at(layer, 4))
                        act.wait_ge(gated_ok.sem, gated_ok.at(layer, n))
                        fn(GATE[:], src, ACT.Sigmoid).then_inc(gate_ok.sem, 1)
                        act.wait_ge(gate_ok.sem, gate_ok.at(layer, n + 1))
                        act.sem_inc(bank_free[pair].sem, 1)
                    if what == "wout":
                        y_out(layer, 1, u - 60, pair, g, SQM)

                    if 5 <= u <= 10:
                        act.wait_ge(conv_ok.sem, conv_ok.at(layer, u - 4))
                        t0 = 2 * (u - 5)
                        fn(XBC[:, t0:t0 + 2, :], XBC[:, t0:t0 + 2, :], ACT.Silu).then_inc(xbc_ok.sem, 1)
                    if u == 4:
                        act.wait_ge(z_ok.sem, z_ok.at(layer, 1))
                        fn(E20[:], E20[:], ACT.Exp, scale=-1.0).then_inc(e_ok.sem, 1)
                        fn(AEXP[:, 0:16], VEC[:, V_ALOG:V_ALOG + 16], ACT.Exp).then_inc(aexp_ok.sem, 1)
                    if u == 14:
                        act.wait_ge(cb_ps.sem, cb_ps.at(layer, 1))
                        fn(CB[:], PS[:, 6:8, 0:384], ACT.Copy).then_inc(cb_ok.sem, 1)
                    if u == 15:
                        act.wait_ge(yp32_ok.sem, yp32_ok.at(layer, 1))
                        fn(YPH[:], SCF[0][:], ACT.Copy).then_inc(yph_ok.sem, 1)
                    for q in range(4):
                        if u == 17 + 2 * q:
                            act.wait_ge(seg_ok.sem, seg_ok.at(layer, q + 1))
                            fn(SCR[:, q % 2, :, :], SCR[:, q % 2, :, :], ACT.Exp).then_inc(lm_ok.sem, 1)
                    if u == 28:
                        act.wait_ge(ys_ok.sem, ys_ok.at(layer, 4))
                        fn(SQS[:], SZ[:], ACT.Square).then_inc(ssm_sq.sem, 1)
                    if u == 30:
                        act.wait_ge(fmx_ok.sem, fmx_ok.at(layer, 1))
                        for h in range(HEADS):
                            for it, cs in ((0, slice(0, P)), (1, slice(P, 384))):
                                ins = fn(SCR[:, 1, h, cs], SCR[:, 1, h, cs], ACT.Exp, bias=MX[:, it, h:h + 1],
                                         accum_out=SUM[:, it, h:h + 1])
                        ins.then_inc(fp_ok.sem, 1)
                    if u == 34:
                        for c in range(4):
                            act.wait_ge(ys32_ok.sem, ys32_ok.at(layer, c + 1))
                            fn(YSH[:, 2 * c:2 * c + 2, :], SZ[:, 2 * c:2 * c + 2, :], ACT.Copy).then_inc(ysh_ok.sem, 1)
                    if u == 36:
                        act.wait_ge(fpt_ps.sem, fpt_ps.at(layer, 1))
                        fn(SCR[:, 0, :, :], PS[:, 4:8, 0:384], ACT.Copy).then_inc(fpt_ok.sem, 1)
                    if u == 37:
                        act.wait_ge(fo_ps.sem, fo_ps.at(layer, 1))
                        fn(YFH[:], quad(4), ACT.Copy).then_inc(yfh_ok.sem, 1)
                    if u == 42:
                        act.wait_ge(ro_ps.sem, ro_ps.at(layer, 1))
                        fn(SCF[0][:], quad(4), ACT.Copy).then_inc(ro_ok.sem, 1)
                    if u == 45:
                        act.wait_ge(rc_ok.sem, rc_ok.at(layer, 1))
                        fn(SCF[1][:], SCF[0][:], ACT.Square).then_inc(rsq_ok.sem, 1)
                    if u == 51:
                        act.wait_ge(yr32_ok.sem, yr32_ok.at(layer, 1))
                        fn(YRH[:], SCF[0][:], ACT.Copy).then_inc(yrh_ok.sem, 1)
                    if u in (54, 56, 58):
                        merged_hi(layer, (u - 54) // 2)

            act.sem_inc(bank_free[0].sem, 1)
            act.sem_inc(bank_free[1].sem, 1)
            act.wait_ge(c_landed, 16)
            fn(CS[:], CS[:], ACT.Silu).then_inc(c_ok, 1)
            split(0, 0, KD)
            split(0, 1, KD)
            act.wait_ge(turned, 1)
            for c in range(4):
                ins = fn(X[:, 2 * c:2 * c + 2, :], PS[:, 4 + c, :].rearrange("p (k t) -> p k t", k=2), ACT.Copy)
            ins.then_inc(x_ready.sem, 4)
            act.wait_ge(turned, 2)
            with act.Fori(0, DEPTH) as layer:
                ffn(layer, 0)
                mixer(layer)
                ffn(layer, 1)
            act.wait_ge(fin_ps, 1)
            act.wait_ge(y_ok.sem, DEPTH * SUBS * 4)
            for tt in range(TT):
                ins = fn(XTOK[:, tt, :], PS[:, 4 + 2 * tt:6 + 2 * tt, :].rearrange("p b c -> p (b c)"), ACT.Copy)
            ins.then_inc(fin_ok, 1)

        @block.vector
        def _(dve):
            chain = Chain(dve, dve_chain, DVE_CHAIN)

            def split(layer, u, kn, cols=COLS, i=0, step=0):
                s = u % 4
                for t in range(1 if u in POOL_SPLITS or cols != COLS else 2):
                    m = 2 * u + t
                    if t == 0 and u - 1 in POOL_SPLITS:
                        dve.wait_ge(w_lo.sem, w_lo.at(layer, m))
                    n = P if cols == COLS else cols
                    dve.wait_ge(w_hi.sem, w_hi.at(layer, m + (1 if cols == COLS else 2) + i * (2 * step)))
                    raw = RAW[:, s, 0:kn * cols].rearrange("p (k n) -> p k n", k=kn)[:, :, t * n:(t + 1) * n]
                    hi = WH[:, m % 4, 0:kn * n].rearrange("p (k n) -> p k n", k=kn)
                    dve.tensor_tensor(WL[:, m % 4, 0:kn * n].rearrange("p (k n) -> p k n", k=kn), raw, hi, ALU.subtract)\
                        .then_inc(w_lo.sem, 1 if cols == COLS else 2)

            def done(layer, u, i=0, step=0):
                dve.wait_ge(w_used.sem, w_used.at(layer, 2 * u + 2 + i * (2 * step)))

            def ada(piece, r, slab):
                acc = ACC[:, bass.ds(piece * ADA_COLS, ADA_COLS)]
                w = slab.rearrange("p (k n) -> p k n", k=2)
                if r == 0:
                    chain(dve.tensor_scalar(acc, w[:, 0, :], CS[:, 0:1], None, ALU.mult))
                else:
                    chain(dve.scalar_tensor_tensor(acc, w[:, 0, :], CS[:, 2 * r:2 * r + 1], acc, ALU.mult, ALU.add))
                dve.scalar_tensor_tensor(acc, w[:, 1, :], CS[:, 2 * r + 1:2 * r + 2], acc, ALU.mult, ALU.add)\
                    .then_inc(ada_used.sem, 1)

            def ada_step(layer, sub, piece, r):
                n = (sub * ADA_STEPS + r) // 2 + 1
                dve.wait_ge(ada_landed[r % 2].sem, ada_landed[r % 2].at(layer, n * 16 + piece * 32))
                dve.wait_ge(ada_used.sem, ada_used.at(layer, sub * ADA_STEPS + r + piece * 4))
                ada(piece, r, SLAB[:, r % 2, :])

            def newton(layer, which, n, scale, eps, as_rows=False):
                v, r, t = NV[:, 0:n], RSTD[:, 0:n], NT[:, 0:n]
                dve.wait_ge(stat_ps.sem, stat_ps.at(layer, which + 1))
                src = PS[:, 4:6, 0:n // 2]
                if as_rows:
                    chain(dve.tensor_tensor(DG[:], PS[:, 4, 0:T].rearrange("p (a b) -> p a b", a=TT),
                                            ident.unsqueeze(1).to_broadcast([P, TT, P]), ALU.mult))
                    chain(dve.tensor_reduce(t, DG[:], AX_X, ALU.add))
                    src, scale = t.unsqueeze(2), scale * P
                chain(dve.tensor_scalar(v.rearrange("p (a b) -> p a b", a=2), src, scale, eps, ALU.mult, ALU.add))
                chain(dve.tensor_scalar(r.bitcast(I32), v.bitcast(I32), -0.5, float(0x5f3759df), ALU.mult, ALU.add))
                for it in range(3):
                    chain(dve.scalar_tensor_tensor(t, r, -0.5, r, ALU.mult, ALU.mult))
                    chain(dve.scalar_tensor_tensor(t, t, 1.0, v, ALU.mult, ALU.mult))
                    ins = dve.scalar_tensor_tensor(r, t, 1.5, r, ALU.add, ALU.mult)
                    if it < 2:
                        chain(ins)
                ins.then_inc(rstd_ok.sem, 1)

            def rows(n):
                return PS[:, 6, 0:T].unsqueeze(1).to_broadcast([P, n, T])

            def pre(layer, s):
                dve.wait_ge(mod_ps.sem, mod_ps.at(layer, s + 1))
                b = V_BADA + 24 * s
                chain(dve.tensor_tensor(MODV[:, 0:16], PS[:, 7, 0:16], VEC[:, b:b + 16], ALU.add))
                dve.scalar_tensor_tensor(AMOD[:], MODV[:, 8:16], 1.0, VEC[:, V_PRE + 8 * s:V_PRE + 8 * s + 8],
                                         ALU.add, ALU.mult).then_inc(mod_ok.sem, 1)
                newton(layer, ST_PRE[s], 2, 1.0 / D, RMS_EPS, as_rows=True)
                dve.wait_ge(rb_ps.sem, rb_ps.at(layer, ST_PRE[s] + 1))
                for c in range(4):
                    cc = slice(2 * c, 2 * c + 2)
                    dve.wait_ge(xa_ok.sem, xa_ok.at(layer, 4 * s + c + 1))
                    dve.tensor_tensor(H32[:, cc, :], H32[:, cc, :], rows(2), ALU.mult).then_inc(h32_ok.sem, 1)
                    if c:
                        to_lo(layer, H_PRE[s], c - 1)
                to_lo(layer, H_PRE[s], 3)
                dve.wait_ge(modg_ps.sem, modg_ps.at(layer, s + 1))
                chain(dve.tensor_tensor(MODV[:, 16:24], PS[:, 5, 16:24], VEC[:, b + 16:b + 24], ALU.add))
                dve.scalar_tensor_tensor(GMOD[:], MODV[:, 16:24], 0.5 if s != 1 else 1.0,
                                         VEC[:, V_POST + 8 * s:V_POST + 8 * s + 8], ALU.mult, ALU.mult)\
                    .then_inc(gmod_ok.sem, 1)

            def to_lo(layer, n0, c):
                dve.wait_ge(hh_ok.sem, hh_ok.at(layer, n0 + c + 1))
                for k in (2 * c, 2 * c + 1):
                    ins = dve.scalar_tensor_tensor(HL[:, k, :], H32[:, k, :], MODV[:, k:k + 1], HH[:, k, :],
                                                   ALU.add, ALU.subtract)
                ins.then_inc(hl_ok.sem, 1)

            def merged_lo(layer, c):
                cc = slice(2 * c, 2 * c + 2)
                dve.wait_ge(mh_ok.sem, mh_ok.at(layer, c + 1))
                dve.tensor_tensor(YSL[:, cc, :], Y[:, cc, :], YSH[:, cc, :], ALU.subtract).then_inc(ml_ok.sem, 1)

            def post(layer, s):
                newton(layer, ST_POST[s], 2, 1.0 / D, RMS_EPS)
                dve.wait_ge(rb_ps.sem, rb_ps.at(layer, ST_POST[s] + 1))
                for c in range(4):
                    cc = slice(2 * c, 2 * c + 2)
                    dve.wait_ge(y_ok.sem, y_ok.at(layer, 4 * s + c + 1))
                    chain(dve.tensor_tensor(Y[:, cc, :], Y[:, cc, :], rows(2), ALU.mult))
                    dve.tensor_tensor(X[:, cc, :], X[:, cc, :], Y[:, cc, :], ALU.add).then_inc(x_ready.sem, 1)
                dve.wait_ge(x_ready.sem, x_ready.at(layer, 4 * s + 4 + 4))

            def ffn(layer, f):
                ub, s = UB_FFN[f], 2 * f
                pre(layer, s)

                def gate_unit(i, r, kn_next, piece=None):
                    split(layer, ub + r + 2, kn_next, i=i, step=4)
                    if piece is not None:
                        ada_step(layer, s, piece, r % 4)

                def up_unit(i, r, kn_next, piece=None):
                    split(layer, ub + r + 2, kn_next, i=i, step=4)
                    if piece is not None:
                        ada_step(layer, s, piece, r % 4)
                    done(layer, ub + r, i, 4)
                    j = f * IN_PAIRS + r // 2
                    b = (r // 2) % 2
                    dve.wait_ge(gs_ok.sem, gs_ok.at(layer, j + 1 + i * 2))
                    dve.wait_ge(al_ok.sem, al_ok.at(layer, j - 1 + i * 2))
                    dve.tensor_tensor(A32[:, b, :, :], GS[:, b, :, :], PS[:, 2:4, 0:T], ALU.mult).then_inc(a32_ok.sem, 1)
                    dve.wait_ge(a32_ok.sem, a32_ok.at(layer, j + 1 + i * 2))
                    dve.sem_inc(bank_free[1].sem, 1)

                with dve.Fori(0, 4) as i:
                    chain.enter_loop(i, 4)
                    for r in (0, 2):
                        gate_unit(i, r, KD, piece=i)
                        up_unit(i, r + 1, KD, piece=i)
                chain.leave_loop(4)
                for r in (16, 18, 20):
                    gate_unit(0, r, KD if r < 20 else OUT_SPLIT[0])
                    up_unit(0, r + 1, KD if r < 20 else OUT_SPLIT[1])
                for r in range(22, FFN_UNITS):
                    if r + 2 < FFN_UNITS:
                        split(layer, ub + r + 2, OUT_SPLIT[(r - 20) % 4])
                    else:
                        split(layer, ub + r + 2, KD)
                post(layer, s)

            def mixer(layer):
                pre(layer, 1)
                for u, (what, col, kn, cols) in enumerate(MIX):
                    g = UB_MIX + u
                    pair = u % 2
                    src = PS[:, 2 * pair:2 * pair + 2, 0:T]
                    _, _, kn_next, cols_next = MIX[u + 2] if u + 2 < MIX_UNITS else (None, None, KD, COLS)
                    if u != 59:
                        split(layer, g + 2, kn_next, cols_next)
                    if what == "dt":
                        done(layer, g)
                        chain(dve.tensor_tensor(Z20[:, :, 0:16], PS[:, 0:2, 0:16],
                                                VEC[:, V_B20:V_B20 + 16].unsqueeze(1).to_broadcast([P, 2, 16]), ALU.add))
                        dve.sem_inc(bank_free[0].sem, 1)
                        chain(dve.tensor_scalar(Z20[:, :, 0:16], Z20[:, :, 0:16], -1.0, None, ALU.mult))
                    if what == "ff":
                        done(layer, g)
                        chain(dve.tensor_tensor(Z20[:, :, 16:20], PS[:, 2:4, 0:4],
                                                VEC[:, V_B20 + 16:V_B20 + 20].unsqueeze(1).to_broadcast([P, 2, 4]), ALU.add))
                        dve.sem_inc(bank_free[1].sem, 1)
                        dve.scalar_tensor_tensor(E20[:], Z20[:], -1.0, Z20[:], ALU.mult, ALU.max).then_inc(z_ok.sem, 1)
                    if what == "xbc":
                        dve.wait_ge(tap0_ok.sem, tap0_ok.at(layer, u - 3))
                        t0 = (col - C_XBC) // P
                        for back in (1, 2, 3):
                            for t in range(2):
                                wcol = V_CW + 12 * (3 - back) + t0 + t
                                ins = dve.scalar_tensor_tensor(
                                    XBC[:, t0 + t, back:T], PS[:, 2 * pair + t, 0:T - back], VEC[:, wcol:wcol + 1],
                                    XBC[:, t0 + t, back:T], ALU.mult, ALU.add)
                                if back < 3:
                                    chain(ins)
                        ins.then_inc(conv_ok.sem, 1)
                        dve.wait_ge(conv_ok.sem, conv_ok.at(layer, u - 3))
                        dve.sem_inc(bank_free[pair].sem, 1)
                    if what in ("rq", "rk"):
                        n = u - 28
                        dve.wait_ge(swap_ok.sem, swap_ok.at(layer, n + 1))
                        dst, c0 = (RQ, C_RQ) if what == "rq" else (RK, C_RK)
                        t = (col - c0) // P
                        cos = con(K_COS, T).unsqueeze(1).to_broadcast([P, 2, T])
                        dve.tensor_tensor(dst[:, t:t + 2, :], src, cos, ALU.mult).then_inc(rcos_ok.sem, 1)
                        dve.wait_ge(rcos_ok.sem, rcos_ok.at(layer, n + 1))
                        dve.sem_inc(bank_free[pair].sem, 1)
                    if what in BRANCHES:
                        n = (u - 21) // 2 if u < 28 else 4 + (u - 37) // 2
                        p = col // COLS
                        done(layer, g)
                        dve.wait_ge(gate_ok.sem, gate_ok.at(layer, n + 1))
                        merged = Y[:, 2 * p:2 * p + 2, :]
                        if what == "pool":
                            dve.tensor_tensor(merged, GATE[:], src, ALU.mult).then_inc(gated_ok.sem, 1)
                            dve.wait_ge(gated_ok.sem, gated_ok.at(layer, n + 1))
                            dve.sem_inc(bank_free[pair].sem, 1)
                        else:
                            dve.tensor_tensor(GATE[:], GATE[:], src, ALU.mult).then_inc(gmul_ok.sem, 1)
                            dve.wait_ge(gmul_ok.sem, gmul_ok.at(layer, n - 3))
                            dve.sem_inc(bank_free[pair].sem, 1)
                    if u in ADA_AT:
                        n = ADA_AT.index(u)
                        ada_step(layer, 1, n // 4, n % 4)
                    if u in (54, 56, 58):
                        merged_lo(layer, (u - 54) // 2)
                    if u == 59:
                        merged_lo(layer, 3)
                        split(layer, g + 2, kn_next, cols_next)

                    if u == 5:
                        dve.wait_ge(e_ok.sem, e_ok.at(layer, 1))
                        chain(dve.tensor_scalar(S20[:], E20[:], 2.0, None, ALU.add))
                        chain(dve.reciprocal(S20[:], S20[:]))
                        chain(dve.tensor_tensor(S20[:], S20[:], E20[:], ALU.mult))
                        chain(dve.tensor_tensor(Q20[:], S20[:], S20[:], ALU.mult))
                        chain(dve.tensor_scalar(R20[:], Q20[:], 1.0 / 15, None, ALU.mult))
                        for odd in (13, 11, 9, 7, 5, 3):
                            chain(dve.scalar_tensor_tensor(R20[:], R20[:], 1.0 / odd, Q20[:], ALU.add, ALU.mult))
                        chain(dve.scalar_tensor_tensor(R20[:], R20[:], 1.0, S20[:], ALU.add, ALU.mult))
                        chain(dve.tensor_scalar(R20[:], R20[:], 2.0, None, ALU.mult))
                        chain(dve.scalar_tensor_tensor(R20[:], Z20[:], 0.0, R20[:], ALU.min, ALU.subtract))
                        chain(dve.tensor_scalar(DTV[:], R20[:, :, 0:16], -1.0, None, ALU.mult))
                        dve.wait_ge(aexp_ok.sem, aexp_ok.at(layer, 1))
                        dve.tensor_tensor(DA[:], R20[:], AEXP[:].unsqueeze(1).to_broadcast([P, 2, 20]), ALU.mult)\
                            .then_inc(da_ok.sem, 1)
                    if u == 9:
                        dve.wait_ge(acum_ps.sem, acum_ps.at(layer, 1))
                        dve.tensor_copy(ACUM[:], PS[:, 4:6, 0:20]).then_inc(acum_ok.sem, 1)
                    if u == 10:
                        dve.wait_ge(pwin_ok.sem, pwin_ok.at(layer, 1))
                        for gg in range(HEADS):
                            buf = PW if gg % 2 == 0 else SCF[1]
                            ins = dve.scalar_tensor_tensor(buf[:, gg, :], buf[:, gg, :], 1.0 / 2 ** (gg + 1), PU[:, gg, :],
                                                           ALU.mult, ALU.subtract)
                        ins.then_inc(pooled_ok.sem, 1)
                    if u == 14:
                        dve.wait_ge(pmix_ps.sem, pmix_ps.at(layer, 1))
                        for gg in range(HEADS):
                            ins = dve.tensor_scalar(SCF[0][:, gg, :], quad(4)[:, gg, :], VEC[:, V_PSC + gg:V_PSC + gg + 1],
                                                    None, ALU.mult)
                        ins.then_inc(yp32_ok.sem, 1)
                    if u == 16:
                        dve.wait_ge(yph_ok.sem, yph_ok.at(layer, 1))
                        dve.tensor_tensor(YPL[:], SCF[0][:], YPH[:], ALU.subtract).then_inc(ypl_ok.sem, 1)
                    if u == 12:
                        dve.wait_ge(xst_ps.sem, xst_ps.at(layer, 1))
                        for tt in range(TT):
                            ins = dve.tensor_tensor(
                                XDT[:, tt, :].rearrange("p (h d) -> p h d", h=SH),
                                PS[:, 4 + 2 * tt:6 + 2 * tt, :].rearrange("p b (h d) -> p (b h) d", d=SHD),
                                DTV[:, tt, :].unsqueeze(2).to_broadcast([P, SH, SHD]), ALU.mult)
                        ins.then_inc(xdt_ok.sem, 1)
                    for q in range(4):
                        sc = SCR[:, q % 2]
                        if u == 16 + 2 * q:
                            dve.wait_ge(ab_ps.sem, ab_ps.at(layer, q + 1))
                            if q == 0:
                                dve.wait_ge(ypl_ok.sem, ypl_ok.at(layer, 1))
                            for h4 in range(4):
                                h = 4 * q + h4
                                dve.scalar_tensor_tensor(sc[:, h4, 0:T], quad(4)[:, h4, :], ACUM[:, 0, h:h + 1],
                                                         con(K_NEGT, T), ALU.subtract, ALU.add)
                                ins = dve.scalar_tensor_tensor(sc[:, h4, T:384], quad(4)[:, h4, P:T], ACUM[:, 1, h:h + 1],
                                                               con(K_NEGT, P), ALU.subtract, ALU.add)
                            ins.then_inc(seg_ok.sem, 1)
                        if u == 20 + 2 * q:
                            dve.wait_ge(yq_ps.sem, yq_ps.at(layer, q + 1))
                            for j in range(2):
                                t = 2 * q + j
                                ins = dve.scalar_tensor_tensor(XBC[:, t, :], XBC[:, t, :], VEC[:, V_DSK + t:V_DSK + t + 1],
                                                               PS[:, 7, j * T:(j + 1) * T], ALU.mult, ALU.add)
                            ins.then_inc(ydx_ok.sem, 1)
                    if u == 31:
                        newton(layer, ST_SSM, 2, 1.0 / D, RMS_EPS, as_rows=True)
                    if u == 33:
                        dve.wait_ge(rb_ps.sem, rb_ps.at(layer, ST_SSM + 1))
                        for c in range(4):
                            cc = slice(2 * c, 2 * c + 2)
                            chain(dve.tensor_tensor(SZ[:, cc, :], SZ[:, cc, :], rows(2), ALU.mult))
                            for k in (2 * c, 2 * c + 1):
                                ins = dve.tensor_scalar(SZ[:, k, :], SZ[:, k, :], VEC[:, V_SSMN + k:V_SSMN + k + 1],
                                                        None, ALU.mult)
                            ins.then_inc(ys32_ok.sem, 1)
                    if u == 25:
                        dve.wait_ge(fab_ps.sem, fab_ps.at(layer, 1))
                        negf = con(K_NEGF, P).unsqueeze(1).to_broadcast([P, HEADS, P])
                        zneg = con(K_ZERO, T).unsqueeze(1).to_broadcast([P, HEADS, T])
                        dve.tensor_tensor(SCR[:, 0, :, 0:P], negf, quad(4)[:, :, 0:P], ALU.subtract)
                        dve.tensor_tensor(SCR[:, 0, :, P:384], zneg, quad(4), ALU.subtract).then_inc(fx_ok.sem, 1)
                        dve.wait_ge(fx_ok.sem, fx_ok.at(layer, 1))
                    if u == 35:
                        dve.wait_ge(ysh_ok.sem, ysh_ok.at(layer, 4))
                        dve.tensor_tensor(YSL[:], SZ[:], YSH[:], ALU.subtract).then_inc(ysl_ok.sem, 1)
                    if u == 29:
                        dve.wait_ge(fs_ps.sem, fs_ps.at(layer, 1))
                        for h in range(HEADS):
                            ins = dve.scalar_tensor_tensor(SCR[:, 1, h, :], PS[:, 4 + h, 0:384], P ** -0.5, SCR[:, 0, h, :],
                                                           ALU.mult, ALU.add)
                        chain(ins)
                        dve.tensor_reduce(MX[:, 0, :], SCR[:, 1, :, 0:P], AX_X, ALU.max)
                        chain(dve.tensor_reduce(MX[:, 1, :], SCR[:, 1, :, P:384], AX_X, ALU.max))
                        dve.tensor_scalar(MX[:], MX[:], -1.0, None, ALU.mult).then_inc(fmx_ok.sem, 1)
                    if u == 31:
                        dve.wait_ge(fp_ok.sem, fp_ok.at(layer, 1))
                        chain(dve.reciprocal(RIN[:], SUM[:]))
                        dve.tensor_tensor(SCR[:, 1, :, 0:P], SCR[:, 1, :, 0:P],
                                          RIN[:, 0, :].unsqueeze(2).to_broadcast([P, HEADS, P]), ALU.mult)
                        dve.tensor_tensor(SCR[:, 1, :, P:384], SCR[:, 1, :, P:384],
                                          RIN[:, 1, :].unsqueeze(2).to_broadcast([P, HEADS, T]), ALU.mult)\
                            .then_inc(fpn_ok.sem, 1)
                    if u == 38:
                        dve.wait_ge(yfh_ok.sem, yfh_ok.at(layer, 1))
                        dve.tensor_tensor(YFL[:], quad(4), YFH[:], ALU.subtract).then_inc(yfl_ok.sem, 1)
                    if u == 40:
                        dve.wait_ge(rs_ps.sem, rs_ps.at(layer, 1))
                        dve.wait_ge(dec_landed, 16)
                        dec = con(K_DEC, HEADS * 384).rearrange("p (h c) -> p h c", h=HEADS)
                        dve.tensor_tensor(SCR[:, 1, :, :], PS[:, 4:8, 0:384], dec, ALU.mult).then_inc(rs_ok.sem, 1)
                    if u == 44:
                        dve.wait_ge(rm_ps.sem, rm_ps.at(layer, 1))
                        dve.wait_ge(ro_ok.sem, ro_ok.at(layer, 1))
                        dve.tensor_tensor(SCF[0][:], SCF[0][:], quad(6), ALU.subtract).then_inc(rc_ok.sem, 1)
                    if u == 47:
                        dve.wait_ge(rc_ok.sem, rc_ok.at(layer, 1))
                        newton(layer, ST_RET, 8, 1.0 / P, GN_EPS)
                        dve.wait_ge(rvg_ok.sem, rvg_ok.at(layer, 4))
                        dve.wait_ge(rsq_ok.sem, rsq_ok.at(layer, 1))
                        chain(dve.tensor_tensor(SCF[0][:], SCF[0][:], RG[:], ALU.mult))
                    if u == 50:
                        dve.wait_ge(rb_ps.sem, rb_ps.at(layer, ST_RET + 1))
                        dve.tensor_tensor(SCF[0][:], SCF[0][:], quad(4), ALU.mult).then_inc(yr32_ok.sem, 1)
                    if u == 51:
                        dve.wait_ge(yrh_ok.sem, yrh_ok.at(layer, 1))
                        dve.tensor_tensor(YRL[:], SCF[0][:], YRH[:], ALU.subtract).then_inc(yrl_ok.sem, 1)
                post(layer, 1)

            dve.sem_inc(w_lo.sem, w_lo.before)
            dve.sem_inc(w_used.sem, w_used.before)
            dve.sem_inc(gated_ok.sem, gated_ok.before)
            dve.sem_inc(ada_used.sem, 2)
            dve.sem_inc(a32_ok.sem, a32_ok.before)
            dve.sem_inc(al_ok.sem, al_ok.before)
            dve.memset(AEXP[:, 16:20], 1.0)
            split(0, 0, KD)
            split(0, 1, KD)
            dve.wait_ge(c_ok, 1)
            for piece in range(4):
                if piece == 1:
                    dve.wait_ge(turned, 2)
                    for l in range(DEPTH):
                        ins = dve.tensor_copy(VECS[:, l, 0:192], PS[:, l, 0:192])
                    ins.then_inc(vecs_ok, 1)
                    dve.wait_ge(vecs_ok, 1)
                    dve.wait_ge(x_ready.sem, 4)
                    dve.sem_inc(zero_bank, 1)
                for r in range(4):
                    e = 4 * piece + r
                    dve.wait_ge(first_landed[e % 8], 16 * (e // 8 + 1))
                    if e:
                        dve.wait_ge(ada_used.sem, 2 + e)
                    ada(piece, r, PSLAB[:, e % 8, :])
            with dve.Fori(0, DEPTH) as layer:
                chain.enter_layers(layer)
                chain(dve.tensor_copy(VEC[:], VECS[:, bass.ds(layer, 1), :].rearrange("p a v -> p (a v)")))
                ffn(layer, 0)
                mixer(layer)
                ffn(layer, 1)
                chain.leave_layers()

        @block.gpsimd
        def _(pool):
            chain = Chain(pool, pool_chain, POOL_CHAIN)

            def act_lo(layer, f, i, r):
                j = f * IN_PAIRS + r
                pool.wait_ge(ah_ok.sem, ah_ok.at(layer, j + 1 + i * 2))
                pool.sem_inc(passed, 1)
                dst = bass.ds(i * 4 + r * 2, 2)
                pool.tensor_tensor(AL[:, dst, :], A32[:, r % 2, :, :], AH[:, dst, :], ALU.subtract).then_inc(al_ok.sem, 1)

            def sum_squares(layer, s, sq):
                pool.wait_ge(post_sq.sem, post_sq.at(layer, 4 * s + 2))
                chain(pool.tensor_tensor(sq[:, 0:2, :], sq[:, 0:2, :], sq[:, 2:4, :], ALU.add))
                pool.wait_ge(post_sq.sem, post_sq.at(layer, 4 * s + 3))
                pool.tensor_tensor(sq[:, 0:2, :], sq[:, 0:2, :], sq[:, 4:6, :], ALU.add).then_inc(sqsum_ok.sem, 1)

            def ffn(layer, f):
                with pool.Fori(0, 5) as i:
                    act_lo(layer, f, i, 0)
                    act_lo(layer, f, i, 1)
                act_lo(layer, f, 0, 10)
                sum_squares(layer, 2 * f, SQ)

            def split_second(layer, u):
                m = 2 * u + 1
                pool.wait_ge(w_hi.sem, w_hi.at(layer, m + 1))
                pool.wait_ge(w_lo.sem, w_lo.at(layer, m))
                pool.sem_inc(passed, 1)
                raw = RAW[:, u % 4, :].rearrange("p (k n) -> p k n", k=KD)[:, :, P:2 * P]
                hi = WH[:, m % 4, :].rearrange("p (k n) -> p k n", k=KD)
                pool.tensor_tensor(WL[:, m % 4, :].rearrange("p (k n) -> p k n", k=KD), raw, hi, ALU.subtract)\
                    .then_inc(w_lo.sem, 1)

            def pool_windows(layer):
                W2 = SCF[1]
                pool.wait_ge(pu_ok.sem, pu_ok.at(layer, 2))

                def widen(dst, src, g0, w):
                    pool.tensor_tensor(dst[:, g0:HEADS, w:T], src[:, g0:HEADS, w:T], src[:, g0:HEADS, 0:T - w], ALU.add)
                    chain(pool.tensor_copy(dst[:, g0:HEADS, 0:w], src[:, g0:HEADS, 0:w]))

                widen(PW, PU, 0, 1)
                widen(W2, PW, 1, 2)
                widen(PW, W2, 2, 4)
                widen(W2, PW, 3, 8)
                fix = con(K_FIX, 64).rearrange("p (g t) -> p g t", g=4)
                for g in range(HEADS):
                    buf = PW if g % 2 == 0 else W2
                    ins = pool.tensor_tensor(buf[:, g, 0:16], buf[:, g, 0:16], fix[:, g, :], ALU.mult)
                ins.then_inc(pwin_ok.sem, 1)

            def masked_products(layer, q):
                pool.wait_ge(lm_ok.sem, lm_ok.at(layer, q + 1))
                if q == 0:
                    pool.wait_ge(cb_ok.sem, cb_ok.at(layer, 1))
                sc = SCR[:, q % 2]
                pool.tensor_tensor(sc, sc, CB[:, q // 2, :].unsqueeze(1).to_broadcast([P, 4, 384]), ALU.mult)\
                    .then_inc(m_ok.sem, 1)

            def ssd_gate(layer, q):
                pool.wait_ge(ydx_ok.sem, ydx_ok.at(layer, q + 1))
                if q == 0:
                    pool.wait_ge(sz_ok.sem, sz_ok.at(layer, 4))
                pool.tensor_tensor(SZ[:, 2 * q:2 * q + 2, :], SZ[:, 2 * q:2 * q + 2, :], XBC[:, 2 * q:2 * q + 2, :],
                                   ALU.mult).then_inc(ys_ok.sem, 1)

            def rotate(layer, n):
                dst = RQ if n < 2 else RK
                t = 2 * (n % 2)
                pool.wait_ge(swap_ok.sem, swap_ok.at(layer, n + 1))
                chain(pool.tensor_tensor(SWAP[:], SWAP[:], con(K_SIN, T).unsqueeze(1).to_broadcast([P, 2, T]), ALU.mult))
                pool.wait_ge(rcos_ok.sem, rcos_ok.at(layer, n + 1))
                pool.tensor_tensor(dst[:, t:t + 2, :], dst[:, t:t + 2, :], SWAP[:], ALU.add).then_inc(rot_ok.sem, 1)

            with pool.Fori(0, DEPTH) as layer:
                chain.enter_layers(layer)
                ffn(layer, 0)
                pool_windows(layer)
                for u in POOL_SPLITS:
                    split_second(layer, u)
                masked_products(layer, 0)
                masked_products(layer, 1)
                ssd_gate(layer, 0)
                masked_products(layer, 2)
                ssd_gate(layer, 1)
                masked_products(layer, 3)
                ssd_gate(layer, 2)
                ssd_gate(layer, 3)
                for n in range(4):
                    rotate(layer, n)
                for n in range(12):
                    p = n % 4
                    pool.wait_ge(gmul_ok.sem, gmul_ok.at(layer, n + 1))
                    pool.tensor_tensor(Y[:, 2 * p:2 * p + 2, :], Y[:, 2 * p:2 * p + 2, :], GATE[:], ALU.add)\
                        .then_inc(gated_ok.sem, 1)
                sum_squares(layer, 1, SQM)
                ffn(layer, 1)
                chain.leave_layers()


DVE_CHAIN = 205
POOL_CHAIN = 11

_INS = ["x", "c", "w_ada", "b_ada", "norm_pre", "norm_post", "w_ffn_in", "w_ffn_out", "w_in", "b_forget", "pool_w",
        "pool_scale", "conv_w", "conv_b", "dt_bias", "a_log", "d_skip", "ssm_norm", "w_ret_out", "w_pool_out",
        "w_ssm_out", "w_fox_out", "w_out"]


def kernel(**inputs):
    import concourse.bacc as _bacc
    from concourse.bass_utils import run_bass_kernel_spmd as _run

    nc = _bacc.Bacc("TRN2", target_bir_lowering=False, num_devices=1)
    arrays, args = {}, []
    for name in _INS:
        a = np.ascontiguousarray(inputs[name])
        arrays[f"in_{name}"] = a
        args.append(nc.dram_tensor(f"in_{name}", a.shape, mybir.dt.from_np(a.dtype), kind="ExternalInput").ap())
    table = constant_table()
    arrays["in_consts"] = table
    args.append(nc.dram_tensor("in_consts", table.shape, F32, kind="ExternalInput").ap())
    args.append(nc.dram_tensor("out", (1, T, D), F32, kind="ExternalOutput").ap())
    build(nc, *args)
    r = _run(nc, [arrays], core_ids=[0])
    return r.results[0]["out"]
```
